# Optimizing a Trainium2 kernel written in Bass

```python
import jax, jax.numpy as jnp
from jax import lax
import numpy as np

D_MODEL = 1024
BATCH = 1
SEQ = 512
DEPTH = 2

N_META = 16
BLOCK_Q = 128
N_HEADS_SB = 8
N_HEADS_FOX = 8
HEAD_DIM = D_MODEL // (N_HEADS_SB + N_HEADS_FOX)
D_SB = N_HEADS_SB * HEAD_DIM
D_FOX = N_HEADS_FOX * HEAD_DIM
D_IN_ATTN = 3 * D_SB + 3 * D_FOX + N_HEADS_FOX
D_FF = 2816
POOL_WINDOWS = (2, 4, 8, 16)
N_POOL_GROUPS = len(POOL_WINDOWS)
POOL_GROUP = D_MODEL // N_POOL_GROUPS
RMS_EPS = 1e-6
N_EVEN = (DEPTH + 1) // 2
N_ODD = DEPTH // 2

kernel_name = "hybrid_stickbreak_fox_pool_macaron"

def rms_norm(x, g):
    xf = x.astype(jnp.float32)
    y = xf * lax.rsqrt(jnp.mean(xf * xf, axis=-1, keepdims=True) + RMS_EPS)
    return (y * g.astype(jnp.float32)).astype(x.dtype)

def swiglu(h, w_in, w_out):
    u = h @ w_in
    gate, up = u[..., :D_FF], u[..., D_FF:]
    return (jax.nn.silu(gate) * up) @ w_out

def attn_mixer(h, w_in, b_f, w_out):
    B, L, _ = h.shape
    proj = h @ w_in
    offs = np.cumsum([0, D_SB, D_SB, D_SB, D_FOX, D_FOX, D_FOX])

    def heads(i, n):
        t = proj[..., offs[i]:offs[i + 1]]
        return t.reshape(B, L, n, HEAD_DIM).transpose(0, 2, 1, 3)

    qa, ka, va = heads(0, N_HEADS_SB), heads(1, N_HEADS_SB), heads(2, N_HEADS_SB)
    qb, kb, vb = heads(3, N_HEADS_FOX), heads(4, N_HEADS_FOX), heads(5, N_HEADS_FOX)
    f_logit = proj[..., offs[6]:]
    log_f = jax.nn.log_sigmoid(f_logit.astype(jnp.float32) + b_f.astype(jnp.float32))
    c = jnp.cumsum(log_f, axis=1).transpose(0, 2, 1)

    scale = HEAD_DIM ** -0.5
    starts = [0] + list(range(N_META, L, BLOCK_Q))
    ends = starts[1:] + [L]
    out_sb, out_fox = [], []
    for q0, q1 in zip(starts, ends):
        tpos = jnp.arange(q0, q1)[:, None]
        spos = jnp.arange(q1)[None, :]
        strict = spos < tpos
        causal = spos <= tpos

        z = jnp.einsum('bhqd,bhkd->bhqk', qa[:, :, q0:q1], ka[:, :, :q1]).astype(jnp.float32) * scale
        log_not = jnp.where(strict, jax.nn.log_sigmoid(-z), 0.0)
        rest = lax.cumsum(log_not, axis=3, reverse=True) - log_not
        a_w = jnp.where(strict, jnp.exp(jax.nn.log_sigmoid(z) + rest), 0.0)
        out_sb.append(jnp.einsum('bhqk,bhkd->bhqd', a_w.astype(va.dtype), va[:, :, :q1]))

        s = jnp.einsum('bhqd,bhkd->bhqk', qb[:, :, q0:q1], kb[:, :, :q1]).astype(jnp.float32) * scale
        s = s + c[:, :, q0:q1, None] - c[:, :, None, :q1]
        p = jax.nn.softmax(jnp.where(causal, s, -jnp.inf), axis=-1)
        out_fox.append(jnp.einsum('bhqk,bhkd->bhqd', p.astype(vb.dtype), vb[:, :, :q1]))

    o_sb = jnp.concatenate(out_sb, axis=2).transpose(0, 2, 1, 3).reshape(B, L, D_SB)
    o_fox = jnp.concatenate(out_fox, axis=2).transpose(0, 2, 1, 3).reshape(B, L, D_FOX)
    return jnp.concatenate([o_sb, o_fox], axis=-1) @ w_out

def pool_mixer(h, w_pool, scale):
    B, L, _ = h.shape
    hf = h.astype(jnp.float32).reshape(B, L, N_POOL_GROUPS, POOL_GROUP)
    cs0 = jnp.concatenate([jnp.zeros((B, 1, N_POOL_GROUPS, POOL_GROUP), jnp.float32),
                           jnp.cumsum(hf, axis=1)], axis=1)
    t = jnp.arange(L)
    pooled = []
    for g, w in enumerate(POOL_WINDOWS):
        cg = cs0[:, :, g]
        upper = cg[:, 1:]
        lower = jnp.concatenate([jnp.zeros((B, w - 1, POOL_GROUP), jnp.float32),
                                 cg[:, :L - w + 1]], axis=1)
        cnt = jnp.minimum(t + 1, w).astype(jnp.float32)[None, :, None]
        pooled.append((upper - lower) / cnt - hf[:, :, g])
    p = jnp.stack(pooled, axis=2).astype(h.dtype)
    y = jnp.einsum('blgc,gcd->blgd', p, w_pool).reshape(B, L, D_MODEL)
    return y * scale

def setup_inputs(seed: int = 0) -> dict:
    key = jax.random.key(seed)
    ks = jax.random.split(key, 20)
    f32 = jnp.float32
    nrm = lambda k, shp, s: jax.random.normal(k, shp, f32) * s
    return {
        "x": nrm(ks[0], (BATCH, SEQ, D_MODEL), 1.0),
        "meta_tokens": nrm(ks[1], (N_META, D_MODEL), 1.0),
        "g_ffn1": 1.0 + nrm(ks[2], (DEPTH, D_MODEL), 0.02),
        "w_ffn1_in": nrm(ks[3], (DEPTH, D_MODEL, 2 * D_FF), D_MODEL ** -0.5),
        "w_ffn1_out": nrm(ks[4], (DEPTH, D_FF, D_MODEL), D_FF ** -0.5),
        "g_mix": 1.0 + nrm(ks[5], (DEPTH, D_MODEL), 0.02),
        "g_ffn2": 1.0 + nrm(ks[6], (DEPTH, D_MODEL), 0.02),
        "w_ffn2_in": nrm(ks[7], (DEPTH, D_MODEL, 2 * D_FF), D_MODEL ** -0.5),
        "w_ffn2_out": nrm(ks[8], (DEPTH, D_FF, D_MODEL), D_FF ** -0.5),
        "w_attn_in": nrm(ks[9], (N_EVEN, D_MODEL, D_IN_ATTN), D_MODEL ** -0.5),
        "b_forget": 2.0 + nrm(ks[10], (N_EVEN, N_HEADS_FOX), 0.1),
        "w_attn_out": nrm(ks[11], (N_EVEN, D_SB + D_FOX, D_MODEL), (D_SB + D_FOX) ** -0.5),
        "w_pool": nrm(ks[12], (N_ODD, N_POOL_GROUPS, POOL_GROUP, POOL_GROUP), POOL_GROUP ** -0.5),
        "pool_scale": 1.0 + nrm(ks[13], (N_ODD, D_MODEL), 0.02),
        "g_final": 1.0 + nrm(ks[14], (D_MODEL,), 0.02),
    }

def reference(x, meta_tokens, g_ffn1, w_ffn1_in, w_ffn1_out, g_mix, g_ffn2,
              w_ffn2_in, w_ffn2_out, w_attn_in, b_forget, w_attn_out,
              w_pool, pool_scale, g_final):
    B = x.shape[0]
    meta = jnp.broadcast_to(meta_tokens[None].astype(x.dtype), (B, N_META, D_MODEL))
    h = jnp.concatenate([meta, x], axis=1)
    for layer in range(DEPTH):
        h = h + 0.5 * swiglu(rms_norm(h, g_ffn1[layer]), w_ffn1_in[layer], w_ffn1_out[layer])
        u = rms_norm(h, g_mix[layer])
        i = layer // 2
        if layer % 2 == 0:
            h = h + attn_mixer(u, w_attn_in[i], b_forget[i], w_attn_out[i])
        else:
            h = h + pool_mixer(u, w_pool[i], pool_scale[i])
        h = h + 0.5 * swiglu(rms_norm(h, g_ffn2[layer]), w_ffn2_in[layer], w_ffn2_out[layer])
    return rms_norm(h, g_final)[:, N_META:]


_drawn_inputs = setup_inputs


def setup_inputs(seed=0):
    import zlib

    import numpy as np

    out = dict(_drawn_inputs(seed))
    spreads = {}
    factors = {'g_ffn1': 4.646,
     'g_mix': 3.177,
     'g_ffn2': 5.957,
     'b_forget': 49.592,
     'pool_scale': 18.685,
     'g_final': 8.22}
    for name, (base, spread) in spreads.items():
        noise = np.random.default_rng([zlib.crc32(name.encode()), seed]).standard_normal(out[name].shape)
        drawn = base * np.exp(spread * noise) if base else spread * noise
        out[name] = __import__('jax').numpy.asarray(drawn.astype(out[name].dtype))
    for name, factor in factors.items():
        out[name] = (out[name] * factor).astype(out[name].dtype)
    return out
```

```python
import concourse.bass as bass
from concourse import mybir
from contextlib import ExitStack
import numpy as np

F32 = mybir.dt.float32
F32R = mybir.dt.float32r
ACT = mybir.ActivationFunctionType
ALU = mybir.AluOpType
AXX = mybir.AxisListType.X

P = 128
D = 1024
DK = D // P
META = 16
SEQ = 512
T = META + SEQ
HALF = T // 2
FF = 2816
FT = FF // P
BLOCKS = [8, 8, 6]
HD = 64
NH = 8
SCALE = HD ** -0.5
WINDOWS = (2, 4, 8, 16)
EPS = 1e-6
RING = 4
UNIT = 8 * P
AHEAD = 2
QT = 5
MASKED = -3.0e38

G_FFN1, G_MIX, G_FFN2, G_FINAL, G_POOL = (0, 1), (2, 3), (4, 5), 6, 7


class Phase:
    def __init__(self, kind, n0, t0, x0, s0, xg0, gain, which, layer, last, swapped):
        self.kind, self.n0, self.t0, self.x0, self.s0, self.xg0 = kind, n0, t0, x0, s0, xg0
        self.gain, self.which, self.layer, self.last, self.swapped = gain, which, layer, last, swapped
        self.blocks = []


def plan():
    out, n, t, x, s, xg = [], 0, 0, DK, 0, DK
    order = [("ffn", 0, 0, G_MIX[0]), ("attn", 0, 0, G_FFN2[0]), ("ffn", 1, 0, G_FFN1[1]),
             ("ffn", 0, 1, None), ("pool", 0, 1, G_FFN2[1]), ("ffn", 1, 1, None)]
    swapped = False
    for at, (kind, which, layer, gain) in enumerate(order):
        ph = Phase(kind, n, t, x, s, xg, gain, which, layer, at == len(order) - 1, swapped)
        out.append(ph)
        if kind == "ffn":
            f = 0
            for nf in BLOCKS:
                ph.blocks.append((n, t, f, nf))
                n += 2 * nf + DK
                t += nf
                f += nf
        elif kind == "attn":
            n += 24 + DK
            swapped = not swapped
        else:
            n += 4
            swapped = not swapped
        x += DK
        s += 1
        xg += DK if gain is not None else 0
    return out, n


def trunk(nc, x, meta_tokens, g_ffn1, w_ffn1_in, w_ffn1_out, g_mix, g_ffn2, w_ffn2_in, w_ffn2_out,
          w_attn_in, b_forget, w_attn_out, w_pool, pool_scale, g_final, out):
    PHASES, UNITS = plan()
    w_in = (w_ffn1_in, w_ffn2_in)
    w_out = (w_ffn1_out, w_ffn2_out)
    ctx = ExitStack()
    with ctx:
        def sb(name, shape, dt=F32, at=ctx):
            return at.enter_context(nc.sbuf_tensor(name, shape, dt))

        def sem(name):
            return ctx.enter_context(nc.semaphore(name))

        h = sb("h", [P, DK, T])
        b0_hi = sb("b0_hi", [P, DK, T], F32R)
        b0_lo = sb("b0_lo", [P, DK, T], F32R)
        raw = [sb(f"raw{i}", [P, UNIT]) for i in range(RING)]
        w_hi = [sb(f"w_hi{i}", [P, UNIT], F32R) for i in range(RING)]
        w_lo = [sb(f"w_lo{i}", [P, UNIT], F32R) for i in range(RING)]
        rinv = sb("rinv", [P, T])
        sumsq = sb("sumsq", [P, T])
        gains = sb("gains", [P, 8 * DK])
        ident = sb("ident", [P, P])
        ones = sb("ones", [P, P])
        neg_tri = sb("neg_tri", [P, P])
        neg_ones = sb("neg_ones", [P, P])
        causal = sb("causal", [P, P])
        eps_col = sb("eps_col", [P, 1])
        sq = sb("sq", [P, T])
        qkv_scale = sb("qkv_scale", [P, 6])
        wf_raw = sb("wf_raw", [P, DK, NH])
        wf_hi = sb("wf_hi", [P, DK, NH], F32R)
        wf_lo = sb("wf_lo", [P, DK, NH], F32R)
        bf_col = sb("bf_col", [NH, 1])
        early = ExitStack()
        b1_hi = sb("b1_hi", [P, DK, T], F32R, early)
        b1_lo = sb("b1_lo", [P, DK, T], F32R, early)
        gate = sb("gate", [P, T], F32, early)
        silu = sb("silu", [P, T], F32, early)
        hid = sb("hid", [P, T], F32, early)
        x_in = sb("x_in", [P, SEQ // P, D], F32, early)
        meta_in = sb("meta_in", [META, D], F32, early)
        gain_rows = sb("gain_rows", [8 * DK, P], F32, early)
        y_out = x_in
        win_a = x_in[:, 0, 0:T]
        win_b = x_in[:, 1, 0:T]
        un = x_in[:, 2, 0:T]
        pooled = x_in[:, 3, 0:T]
        early.close()
        late = ExitStack()
        qkv = sb("qkv", [P, 24, T], F32, late)
        v_tok = sb("v_tok", [P, 2, QT, SEQ], F32, late)
        sb_q = [sb(f"sb_q{i}", [HD, T], F32, late) for i in range(2)]
        sb_k = [sb(f"sb_k{i}", [HD, T], F32, late) for i in range(2)]
        fx_q = [sb(f"fx_q{i}", [HD + 2, T], F32, late) for i in range(2)]
        fx_k = [sb(f"fx_k{i}", [HD + 2, T], F32, late) for i in range(2)]
        head_v = [sb(f"head_v{i}", [P, 2, QT, HD], F32, late) for i in range(2)]
        stats = sb("stats", [P, 2, 4], F32, late)
        turned_p = sb("turned_p", [P, QT, P], F32, late)
        late.close()
        spare = [qkv[:, (8 if i < 4 else 16) + i, :] for i in range(8)]
        log1p = spare[0:2]
        softplus = spare[2:4]
        weight = spare[4:6]
        stick = spare[6]
        probs = [spare[7], sq]
        fg, fg_abs, fg_sum, fg_neg, fg_one = (t[0:NH, :] for t in (sb_q[0], sb_k[0], sb_q[1], sb_k[1], fx_q[0]))
        c_dram = nc.dram_tensor("c_dram", [2, NH, T], F32).ap()
        B = ((b0_hi, b0_lo), (b1_hi, b1_lo))

        psum = [ctx.enter_context(nc.psum_tensor(f"pair{i}", [P, 2, 512], F32)) for i in range(4)]

        landed = [sem(f"landed{i}") for i in range(RING)]
        hi_ready = sem("hi_ready")
        lo_ready = sem("lo_ready")
        unit_done = sem("unit_done")
        drained = sem("drained")
        silu_ready = sem("silu_ready")
        hid_ready = sem("hid_ready")
        act_hi_ready = sem("act_hi_ready")
        act_ready = sem("act_ready")
        xg_hi_ready = sem("xg_hi_ready")
        xg_ready = sem("xg_ready")
        sq_ready = sem("sq_ready")
        sq_added = sem("sq_added")
        sums_done = sem("sums_done")
        root_ready = sem("root_ready")
        rinv_ready = sem("rinv_ready")
        x_landed = sem("x_landed")
        rows_landed = sem("rows_landed")
        consts = sem("consts")
        consts2 = sem("consts2")
        gains_t = sem("gains_t")
        gains_ready = sem("gains_ready")
        turned = sem("turned")
        x_drained = sem("x_drained")
        zeroed = sem("zeroed")
        final_done = sem("final_done")
        y_turned = sem("y_turned")
        y_scaled = sem("y_scaled")
        y_stored = sem("y_stored")
        final_r = sem("final_r")
        scaled = sem("scaled")
        pool_ready = sem("pool_ready")
        pool_hi = sem("pool_hi")
        pool_split = sem("pool_split")
        pool_step = sem("pool_step")
        pool_added = sem("pool_added")
        POOL_STEPS = [0]
        for m in range(DK):
            POOL_STEPS.append(POOL_STEPS[-1] + 1 + int(np.log2(WINDOWS[m * P * len(WINDOWS) // D])))
        FINAL_X = PHASES[-1].x0

        def xg_base(ph):
            return ph.xg0

        (fg_landed, wf_split, fg_mm, fg_step, fg_act, c_stored, vt_turned, vt_out, aug_ones,
         z_done, abs_done, exp_done, ln_done, sp_done, sp_masked, sticks_done, w_done, w_masked, sb_pv,
         s_done, s_masked, max_done, p_exp, p_inv, p_done, p_turned, pt_out, fx_pv, stick_ready,
         o_hi, o_split, v_pad) = (sem(n) for n in (
             "fg_landed wf_split fg_mm fg_step fg_act c_stored vt_turned vt_out aug_ones "
             "z_done abs_done exp_done ln_done sp_done sp_masked sticks_done w_done w_masked sb_pv "
             "s_done s_masked max_done p_exp p_inv p_done p_turned pt_out fx_pv stick_ready "
             "o_hi o_split v_pad").split())
        tp_last = sem("tp_last")
        staged = [sem(f"staged{e}") for e in range(2)]

        block = ctx.enter_context(nc.Block())

        def halves(ph_last):
            if ph_last:
                return [(0, 0, SEQ, META)]
            return [(0, 0, HALF, 0), (1, 0, HALF, HALF)]

        def pair_of(i, last=False):
            return psum[i][:, 0, :] if last else psum[i][:, :, 0:HALF]

        def tok(ap, last=False):
            return ap[:, META:T] if last else ap.rearrange("p (a b) -> p a b", a=2)

        def o_base(hp, g):
            return 6 * hp + 2 * (g // 5) + (1 if g % 5 == 4 else 0)

        def flat(pair):
            return pair[:, :, :].rearrange("p a b -> p (a b)")

        def key_tile(jt):
            return jt * P, min(P, T - jt * P), T - jt * P

        def query_tile(it):
            return (0, META, META) if it == 0 else (META + (it - 1) * P, P, META + it * P)

        def s_psum(it):
            return flat(psum[2]) if it % 2 == 0 else psum[1][:, 1, :]

        def stage_heads(sp, ph):
            def stage(hp, e):
                rows = slice(HD * e, HD * (e + 1))
                head = 2 * hp + e

                def put(dst, src):
                    sp.dma_start(dst, src).then_inc(staged[e], 16)

                put(sb_q[e][:, :], qkv[rows, bass.ds(hp, 1), :].rearrange("p a t -> p (a t)"))
                put(sb_k[e][:, :], qkv[rows, bass.ds(hp + 4, 1), :].rearrange("p a t -> p (a t)"))
                put(fx_q[e][0:HD, :], qkv[rows, bass.ds(hp + 12, 1), :].rearrange("p a t -> p (a t)"))
                put(fx_k[e][0:HD, :], qkv[rows, bass.ds(hp + 16, 1), :].rearrange("p a t -> p (a t)"))
                put(fx_q[e][HD + 1:HD + 2, :], c_dram[0, bass.ds(head, 1), :])
                put(fx_k[e][HD:HD + 1, :], c_dram[1, bass.ds(head, 1), :])
                for kind in range(2):
                    put(head_v[e][:, kind, :, :], v_tok[:, kind, :, bass.ds(head * HD, HD)])

            sp.wait_ge(drained, ph.n0 + 24)
            sp.wait_ge(vt_out, 2 * QT)
            sp.wait_ge(c_stored, 32)
            sp.wait_ge(aug_ones, 4)
            stage(0, 0)
            stage(0, 1)
            with sp.Fori(1, 4) as hp:
                for e in range(2):
                    sp.wait_ge(fx_pv, 10 * hp + 5 * e - 5)
                    stage(hp, e)

        def attn_pe(pe, ph, product, sums, X, A):
            def group(i, first=False):
                for j in range(4):
                    if first and j == 3:
                        pe.wait_ge(root_ready, ph.s0 + 1)
                    if first and j == 2:
                        pe.wait_ge(fg_step, 1)
                    product(ph.n0 + 4 * i + j, j, DK, X, False, xg_ready if first and j == 0 else None, ph.xg0 - DK)
                    if first and j == 0:
                        sums(ph.s0, ph.x0, ph.n0, False)
                        pe.wait_ge(wf_split, 2)
                        for k in range(DK):
                            for w, v in ((wf_hi, 0), (wf_hi, 1), (wf_lo, 0)):
                                for e in range(2):
                                    mm = nc.tensor.matmul(psum[2][0:NH, e, 0:HALF], w[:, k, :],
                                                          X[v][:, k, e * HALF:(e + 1) * HALF],
                                                          start=(k == 0 and w is wf_hi and v == 0),
                                                          stop=(k == DK - 1 and w is wf_lo))
                        mm.then_inc(fg_mm, 1)
            group(0, True)
            with pe.Fori(1, 6) as i:
                group(i)
            pe.wait_ge(drained, ph.n0 + 24)
            for r in range(2 * QT):
                kind, jt = r // QT, r % QT
                t0, kn, _ = key_tile(jt)
                if r >= 8:
                    pe.wait_ge(vt_out, r - 7)
                for a in range(4):
                    mm = nc.tensor.transpose(psum[r % 8 // 2][0:kn, r % 2, a * P:(a + 1) * P],
                                             qkv[:, 12 * kind + 8 + a, t0:t0 + kn], ident[:, :])
                mm.then_inc(vt_turned, 1)
            pe.wait_ge(vt_out, 2 * QT)

            with pe.Fori(0, 4) as hp:
                base = 10 * hp

                def scores(g):
                    e, st = g // 5, g % 5
                    jt = 4 - st
                    k0, kn, nq = key_tile(jt)
                    if st == 0:
                        wait_apart(pe, staged[e], 128 * hp + 128)
                    if g >= 2:
                        wait_apart(pe, w_done, base + (g if st == 0 else g - 1))
                    if jt == 0 and e == 1:
                        pe.wait_ge(o_split, 6 * hp + 3)
                    z = flat(psum[0]) if jt % 2 == 0 else psum[1][:, 0, :]
                    for c0, c1 in ((0, min(nq, 512)), (512, nq)):
                        if c1 > c0:
                            mm = nc.tensor.matmul(z[0:kn, c0:c1], sb_k[e][:, k0:k0 + kn],
                                                  sb_q[e][:, k0 + c0:k0 + c1], start=True, stop=True)
                    mm.then_inc(z_done, 1)
                    q0, qn, nk = query_tile(st)
                    if g >= 2:
                        pe.wait_ge(pt_out, base + (g if st == 0 else g - 1))
                    if st == 4:
                        pe.wait_ge(o_split, 6 * hp + 2 * e + 2)
                    sp_ = s_psum(st)
                    for c0, c1 in ((0, min(nk, 512)), (512, nk)):
                        if c1 > c0:
                            mm = nc.tensor.matmul(sp_[:, c0:c1], fx_q[e][:, q0:q0 + P], fx_k[e][:, c0:c1],
                                                  start=True, stop=True)
                    mm.then_inc(s_done, 1)

                def turn(g):
                    e, st = g // 5, g % 5
                    jt = 4 - st
                    k0, kn, nq = key_tile(jt)
                    z = flat(psum[0]) if jt % 2 == 0 else psum[1][:, 0, :]
                    wait_apart(pe, sp_masked, base + g + 1)
                    pe.wait_ge(stick_ready, base + g + 1)
                    for c0, c1 in ((0, min(nq, 512)), (512, nq)):
                        if c1 > c0:
                            mm = nc.tensor.matmul(z[0:kn, c0:c1], neg_tri[0:kn, 0:kn], softplus[g % 2][0:kn, c0:c1],
                                                  start=False, stop=True, skip_group_check=True)
                    for c0, c1 in ((kn, min(nq, 512)), (512, nq)):
                        if c1 > c0 and jt < 4:
                            mm = nc.tensor.matmul(z[0:kn, c0:c1], neg_ones[:, 0:kn], stick[:, k0 + c0:k0 + c1],
                                                  start=False, stop=True, skip_group_check=True)
                    mm.then_inc(sticks_done, 1)
                    q0, qn, nk = query_tile(st)
                    pe.wait_ge(p_done, base + g + 1)
                    sp_ = s_psum(st)
                    for b in range(st + 1):
                        c1 = min(b * P + P, T)
                        mm = nc.tensor.transpose(sp_[0:c1 - b * P, b * P:b * P + P], probs[g % 2][:, b * P:c1], ident[:, :])
                    mm.then_inc(p_turned, 1)

                def values(g):
                    e, st = g // 5, g % 5
                    jt = 4 - st
                    k0, kn, nq = key_tile(jt)
                    rows = slice(HD * e, HD * (e + 1))
                    if g == 0:
                        pe.wait_ge(o_split, 6 * hp + 1)
                    pe.wait_ge(w_masked, base + g + 1)
                    c0 = META if jt == 0 else 0
                    if jt == 0:
                        nc.tensor.matmul(psum[0][rows, 1, 64:64 + META], head_v[e][0:kn, 0, jt, :],
                                         weight[g % 2][0:kn, 0:META], start=True, stop=True)
                    mm = nc.tensor.matmul(psum[3][rows, 0, k0 + c0 - META:T - META], head_v[e][0:kn, 0, jt, :],
                                          weight[g % 2][0:kn, c0:nq], start=(st == 0), stop=True,
                                          skip_group_check=True)
                    mm.then_inc(sb_pv, 1)
                    pe.wait_ge(pt_out, base + g + 1)
                    q0, qn, nk = query_tile(st)
                    for b in range(st + 1):
                        kb = min(P, nk - b * P)
                        o = psum[2][rows, 1, 256:256 + META] if st == 0 else psum[3][rows, 1, q0 - META:q0 - META + qn]
                        mm = nc.tensor.matmul(o, head_v[e][0:kb, 1, b, :], turned_p[0:kb, b, 0:qn],
                                              start=(b == 0), stop=(b == st), skip_group_check=True)
                    mm.then_inc(fx_pv, 1)

                for g in range(12):
                    if g >= 2:
                        values(g - 2)
                    if g == 5:
                        turn(g - 1)
                    if g < 10:
                        scores(g)
                    if 1 <= g < 11 and g != 5:
                        turn(g - 1)
            n1 = ph.n0 + 24
            pe.wait_ge(o_split, 25)
            with pe.Fori(0, 2) as i:
                for j in range(4):
                    product(n1 + 4 * i + j, j, DK, X, False)

        def attn_act(act, ph, split, tail, root, X, A):
            act.wait_ge(fg_landed, 32)
            nc.scalar.activation(wf_hi[:, :, :], wf_raw[:, :, :], ACT.Copy).then_inc(wf_split, 1)
            for j in range(4):
                split(ph.n0 + j + AHEAD, (j + AHEAD) % RING)
                if j == 0:
                    root(ph.s0, False)
            act.wait_ge(fg_step, 2)
            nc.scalar.activation(fg_abs, fg, ACT.Abs).then_inc(fg_act, 1)
            act.wait_ge(fg_act, 1)
            nc.scalar.activation(fg_abs, fg_abs, ACT.Exp, scale=-1.0).then_inc(fg_act, 1)
            act.wait_ge(fg_act, 2)
            nc.scalar.activation(fg_abs, fg_abs, ACT.Ln, bias=1.0).then_inc(fg_act, 1)
            with act.Fori(1, 6) as i:
                for j in range(4):
                    split(ph.n0 + 4 * i + j + AHEAD, (j + AHEAD) % RING)
            nc.scalar.preload_act_table_set("natural_log_exp_and_others")
            with act.Fori(0, 4) as hp:
                base = 10 * hp

                def stick_log(g):
                    e, st = g // 5, g % 5
                    jt = 4 - st
                    k0, kn, nq = key_tile(jt)
                    z = flat(psum[0]) if jt % 2 == 0 else psum[1][:, 0, :]
                    b = log1p[g % 2][0:kn, 0:nq]
                    act.wait_ge(z_done, base + g + 1)
                    if g >= 2:
                        act.wait_ge(sp_done, base + g - 1)
                    nc.scalar.activation(b, z[0:kn, 0:nq], ACT.Abs).then_inc(abs_done, 1)
                    act.wait_ge(abs_done, base + g + 1)
                    nc.scalar.activation(b, b, ACT.Exp, scale=-1.0).then_inc(exp_done, 1)
                    act.wait_ge(exp_done, base + g + 1)
                    nc.scalar.activation(b, b, ACT.Ln, bias=1.0).then_inc(ln_done, 1)

                def fox_exp(g):
                    st = g % 5
                    q0, qn, nk = query_tile(st)
                    act.wait_ge(max_done, base + g + 1)
                    if g >= 2:
                        act.wait_ge(p_turned, base + g - 1)
                    nc.scalar.activation(probs[g % 2][0:qn, 0:nk], s_psum(st)[0:qn, 0:nk], ACT.Exp,
                                         bias=stats[0:qn, g % 2, 0:1], accum_out=stats[0:qn, g % 2, 1:2]).then_inc(p_exp, 1)

                def stick_weight(g):
                    st = g % 5
                    jt = 4 - st
                    k0, kn, nq = key_tile(jt)
                    z = flat(psum[0]) if jt % 2 == 0 else psum[1][:, 0, :]
                    act.wait_ge(sticks_done, base + g + 1)
                    if g >= 2:
                        act.wait_ge(sb_pv, base + g - 1)
                    nc.scalar.activation(weight[g % 2][0:kn, 0:nq], z[0:kn, 0:nq], ACT.Exp).then_inc(w_done, 1)

                def o_upper(g):
                    e, st = g // 5, g % 5
                    rows = slice(HD * e, HD * (e + 1))
                    if st == 0:
                        wait_apart(act, fx_pv, base + g + 1)
                        nc.scalar.activation(X[0][rows, bass.ds(hp + 4, 1), 0:META].rearrange("p a t -> p (a t)"), psum[2][rows, 1, 256:256 + META],
                                             ACT.Copy).then_inc(o_hi, 1)
                    if st == 4:
                        wait_apart(act, sb_pv, base + g + 1)
                        nc.scalar.activation(X[0][rows, bass.ds(hp, 1), 0:META].rearrange("p a t -> p (a t)"), psum[0][rows, 1, 64:64 + META],
                                             ACT.Copy).then_inc(o_hi, 1)
                    if g == 9:
                        wait_apart(act, fx_pv, base + g + 1)
                        for kind in range(2):
                            nc.scalar.activation(X[0][:, bass.ds(hp + 4 * kind, 1), META:T].rearrange("p a t -> p (a t)"), psum[3][:, kind, :],
                                                 ACT.Copy).then_inc(o_hi, 1)

                for g in range(12):
                    if g == 5:
                        stick_weight(g - 1)
                    if g < 10:
                        stick_log(g)
                    if g >= 2:
                        o_upper(g - 2)
                    if g < 10:
                        fox_exp(g)
                    if 1 <= g < 11 and g != 5:
                        stick_weight(g - 1)
            n1 = ph.n0 + 24
            with act.Fori(0, 2) as i:
                for j in range(4):
                    n = n1 + 4 * i + j
                    split(n + AHEAD, (j + AHEAD) % RING)
                    wait_apart(act, drained, n + 1)
                    tail(4 * i + j, ph.x0 + 4 * i + j, A, ph.gain, 0)

        def attn_dve(dve, ph, split, tail, inverse, X, A):
            dve.wait_ge(wf_split, 1)
            nc.vector.tensor_tensor(wf_lo[:, :, :], wf_raw[:, :, :], wf_hi[:, :, :], ALU.subtract).then_inc(wf_split, 1)

            def group(i, first=False):
                for j in range(4):
                    n = ph.n0 + 4 * i + j
                    split(n + AHEAD, (j + AHEAD) % RING)
                    if first and j == 0:
                        inverse(ph.s0, False)
                        dve.wait_ge(fg_mm, 1)
                        nc.vector.tensor_tensor(tok(fg, False), psum[2][0:NH, :, 0:HALF], tok(rinv[0:NH, :], False),
                                                ALU.mult).then_inc(fg_step, 1)
                    dve.wait_ge(unit_done, n + 1)
                    o = qkv[:, 4 * i + j, :]
                    sc = qkv_scale[:, i:i + 1] if isinstance(i, int) else qkv_scale[:, bass.ds(i, 1)]
                    nc.vector.scalar_tensor_tensor(tok(o, False), pair_of(j), sc, tok(rinv[:, :], False),
                                                   ALU.mult, ALU.mult).then_inc(drained, 1)
                    if first and j == 0:
                        dve.wait_ge(fg_step, 1)
                        nc.vector.tensor_scalar(fg, fg, bf_col[:, 0:1], None, ALU.add).then_inc(fg_step, 1)
                        nc.vector.memset(fg_one, 1.0).then_inc(fg_step, 1)
            group(0, True)
            dve.wait_ge(fg_act, 3)
            dve.wait_ge(fg_step, 3)
            nc.vector.scalar_tensor_tensor(fg, fg, 0.0, fg_abs, ALU.min, ALU.subtract).then_inc(fg_step, 1)
            dve.wait_ge(fg_step, 4)
            nc.vector.tensor_tensor_scan(fg_sum, fg_one, fg, 0.0, ALU.mult, ALU.add).then_inc(fg_step, 1)
            dve.wait_ge(fg_step, 5)
            nc.vector.tensor_scalar(fg_neg, fg_sum, -1.0, None, ALU.mult).then_inc(fg_step, 1)
            with dve.Fori(1, 6) as i:
                group(i)
            dve.wait_ge(v_pad, 1)
            for r in range(2 * QT):
                kind, jt = r // QT, r % QT
                _, kn, _ = key_tile(jt)
                dve.wait_ge(vt_turned, r + 1)
                nc.vector.tensor_copy(v_tok[0:kn, kind, jt, :], psum[r % 8 // 2][0:kn, r % 2, :]).then_inc(vt_out, 1)
            dve.sem_inc(o_split, 1)
            with dve.Fori(0, 4) as hp:
                base = 10 * hp

                def fox_max(g):
                    st = g % 5
                    q0, qn, nk = query_tile(st)
                    sp_ = s_psum(st)
                    dve.wait_ge(s_done, base + g + 1)
                    diag = sp_[0:qn, q0:q0 + qn]
                    nc.vector.tensor_tensor(diag, diag, causal[0:qn, 0:qn], ALU.add).then_inc(s_masked, 1)
                    dve.wait_ge(s_masked, base + g + 1)
                    nc.vector.tensor_reduce(stats[0:qn, g % 2, 0:1], sp_[0:qn, 0:nk], AXX, ALU.max,
                                            negate=True).then_inc(max_done, 1)

                def stick_softplus(g):
                    st = g % 5
                    jt = 4 - st
                    k0, kn, nq = key_tile(jt)
                    z = flat(psum[0]) if jt % 2 == 0 else psum[1][:, 0, :]
                    dve.wait_ge(ln_done, base + g + 1)
                    nc.vector.scalar_tensor_tensor(softplus[g % 2][0:kn, 0:nq], z[0:kn, 0:nq], 0.0, log1p[g % 2][0:kn, 0:nq],
                                                   ALU.max, ALU.add).then_inc(sp_done, 1)

                def fox_probs(g):
                    st = g % 5
                    q0, qn, nk = query_tile(st)
                    dve.wait_ge(p_exp, base + g + 1)
                    nc.vector.reciprocal(stats[0:qn, g % 2, 2:3], stats[0:qn, g % 2, 1:2]).then_inc(p_inv, 1)
                    dve.wait_ge(p_inv, base + g + 1)
                    p = probs[g % 2][0:qn, 0:nk]
                    nc.vector.tensor_scalar(p, p, stats[0:qn, g % 2, 2:3], None, ALU.mult).then_inc(p_done, 1)

                def stick_sum(g):
                    st = g % 5
                    if g >= 1:
                        dve.wait_ge(sticks_done, base + g)
                    if st == 0:
                        nc.vector.memset(stick, 0.0).then_inc(stick_ready, 1)
                    else:
                        k0, kn, nq = key_tile(4 - (st - 1))
                        dve.wait_ge(sp_masked, base + g)
                        nc.vector.tensor_tensor(stick[0:kn, k0:T], stick[0:kn, k0:T], softplus[(g - 1) % 2][0:kn, 0:nq],
                                                ALU.add).then_inc(stick_ready, 1)

                def fox_turned(g):
                    st = g % 5
                    q0, qn, nk = query_tile(st)
                    dve.wait_ge(p_turned, base + g + 1)
                    if g >= 1:
                        dve.wait_ge(fx_pv, base + g)
                    src = s_psum(st)
                    full = min(st + 1, 4)
                    if st == 4:
                        nc.vector.tensor_copy(turned_p[0:META, 4, :], src[0:META, 4 * P:5 * P]).then_inc(tp_last, 1)
                    nc.vector.tensor_copy(turned_p[:, 0:full, 0:qn],
                                          src[:, 0:full * P].rearrange("p (b q) -> p b q", q=P)[:, :, 0:qn]).then_inc(pt_out, 1)

                def o_lower(g):
                    e, st = g // 5, g % 5
                    rows = slice(HD * e, HD * (e + 1))
                    per = o_base(hp, g)
                    if st == 0:
                        dve.wait_ge(o_hi, per + 1)
                        o = lambda v: X[v][rows, bass.ds(hp + 4, 1), 0:META].rearrange("p a t -> p (a t)")
                        nc.vector.tensor_tensor(o(1), psum[2][rows, 1, 256:256 + META], o(0), ALU.subtract).then_inc(o_split, 1)
                    if st == 4:
                        dve.wait_ge(o_hi, per + 1)
                        o = lambda v: X[v][rows, bass.ds(hp, 1), 0:META].rearrange("p a t -> p (a t)")
                        nc.vector.tensor_tensor(o(1), psum[0][rows, 1, 64:64 + META], o(0), ALU.subtract).then_inc(o_split, 1)
                    if g == 9:
                        for kind in range(2):
                            dve.wait_ge(o_hi, per + 2 + kind)
                            o = lambda v: X[v][:, bass.ds(hp + 4 * kind, 1), META:T].rearrange("p a t -> p (a t)")
                            nc.vector.tensor_tensor(o(1), psum[3][:, kind, :], o(0), ALU.subtract).then_inc(o_split, 1)

                for g in range(12):
                    if g == 5:
                        fox_turned(g - 1)
                    if g < 10:
                        stick_sum(g)
                        fox_max(g)
                        stick_softplus(g)
                        fox_probs(g)
                    if g >= 2:
                        o_lower(g - 2)
                    if 1 <= g < 11 and g != 5:
                        fox_turned(g - 1)
            n1 = ph.n0 + 24
            with dve.Fori(0, 2) as i:
                for j in range(4):
                    n = n1 + 4 * i + j
                    m = 4 * i + j
                    split(n + AHEAD, (j + AHEAD) % RING)
                    dve.wait_ge(unit_done, n + 1)
                    hm = tok(h[:, m, :])
                    nc.vector.tensor_tensor(hm, pair_of(j), hm, ALU.add).then_inc(drained, 1)
                    dve.wait_ge(drained, n + 1)
                    tail(m, ph.x0 + m, ph.xg0 + m, A, ph.gain, 0)

        def wait_apart(eng, sem_, count):
            if not isinstance(count, int):
                count = eng.to_reg(count)
            eng.wait_ge(consts, 8)
            eng.wait_ge(sem_, count)

        @block.sync
        def _(sp):
            sp.dma_start(x_in[:, :, :], x[0].rearrange("(a p) d -> p a d", p=P)).then_inc(x_landed, 16)
            sp.dma_start(meta_in[:, :], meta_tokens).then_inc(x_landed, 16)
            sp.dma_start(wf_raw[:, :, :], w_attn_in[0, :, 6 * SEQ:6 * SEQ + NH].rearrange("(k p) c -> p k c", p=P))\
              .then_inc(fg_landed, 16)
            sp.dma_start(bf_col[:, :], b_forget.rearrange("l h -> h l")).then_inc(fg_landed, 16)

            def strip(w, r0, nk, c0, width=P):
                return w[r0:r0 + nk * P, bass.ds(c0, width)].rearrange("(k p) c -> p k c", p=P)

            def dst(j, nk, width=P):
                return raw[j][:, 0:nk * width].rearrange("p (k c) -> p k c", c=width)

            def fetch_to(n, j, nk, src, width=P):
                if not isinstance(n, int) or n >= RING:
                    sp.wait_ge(lo_ready, n - RING + 1)
                sp.dma_start(dst(j, nk, width), src).then_inc(landed[j], 16)

            for ph in PHASES:
                if ph.kind == "ffn":
                    wi, wo = w_in[ph.which][ph.layer], w_out[ph.which][ph.layer]
                    for n0, t0, f0, nf in ph.blocks:
                        def in_group(i):
                            for j in range(4):
                                c = (f0 + 2 * i + j // 2) * P + (j % 2) * FF
                                fetch_to(n0 + 4 * i + j, j, DK, strip(wi, 0, DK, c))
                        in_group(0)
                        with sp.Fori(1, nf // 2) as i:
                            in_group(i)
                        with sp.Fori(0, 2) as i:
                            for j in range(4):
                                fetch_to(n0 + 2 * nf + 4 * i + j, j, nf,
                                         strip(wo, f0 * P, nf, (4 * i + j) * P))
                elif ph.kind == "attn":
                    with sp.Fori(0, 6) as i:
                        for j in range(4):
                            fetch_to(ph.n0 + 4 * i + j, j, DK, strip(w_attn_in[0], 0, DK, (4 * i + j) * P))
                    for i in range(2):
                        for j in range(4):
                            fetch_to(ph.n0 + 24 + 4 * i + j, j, DK, strip(w_attn_out[0], 0, DK, (4 * i + j) * P))
                        if i == 0:
                            stage_heads(sp, ph)
                else:
                    for j in range(4):
                        fetch_to(ph.n0 + j, j, 2, w_pool[0, j].rearrange("(k p) c -> p k c", p=P), 2 * P)
            sp.wait_ge(y_stored, 16 * (SEQ // P))

        def land_wait(eng, n, j):
            eng.wait_ge(landed[j], (n - j) * (16 // RING) + 16)

        @block.scalar
        def _(act):
            act.dma_start(gain_rows[0:16, :], g_ffn1.rearrange("l (m p) -> (l m) p", p=P)).then_inc(rows_landed, 16)
            act.dma_start(gain_rows[16:32, :], g_mix.rearrange("l (m p) -> (l m) p", p=P)).then_inc(rows_landed, 16)
            act.dma_start(gain_rows[32:48, :], g_ffn2.rearrange("l (m p) -> (l m) p", p=P)).then_inc(rows_landed, 16)
            act.dma_start(gain_rows[48:56, :], g_final.rearrange("(m p) -> m p", p=P)).then_inc(rows_landed, 16)
            act.dma_start(gain_rows[56:64, :], pool_scale.rearrange("l (m p) -> (l m) p", p=P)).then_inc(rows_landed, 16)

            def split(n, j):
                if isinstance(n, int) and n >= UNITS:
                    return
                land_wait(act, n, j)
                if not isinstance(n, int) or n >= RING:
                    act.wait_ge(unit_done, n - RING + 1)
                nc.scalar.activation(w_hi[j][:, :], raw[j][:, :], ACT.Copy).then_inc(hi_ready, 1)

            def tail(m, x1, X, gain, lo, last_sq=False):
                v = h[:, m, lo:T]
                if gain is not None:
                    nc.scalar.activation(X[0][:, m, lo:T], v, ACT.Copy,
                                         scale=gains[:, gain * DK + m:gain * DK + m + 1] if isinstance(m, int)
                                         else gains[:, bass.ds(m + gain * DK, 1)]).then_inc(xg_hi_ready, 1)
                wait_apart(act, sq_added, x1)
                nc.scalar.activation(sq[:, lo:T], v, ACT.Square).then_inc(sq_ready, 1)

            def root(s, last):
                act.wait_ge(sums_done, s + 1)
                lo = META if last else 0
                nc.scalar.activation(tok(sq[:, :], last), pair_of(3, last), ACT.Sqrt, scale=1.0 / D,
                                     bias=eps_col[:, 0:1]).then_inc(root_ready, 1)

            act.wait_ge(consts, 8)
            split(0, 0)
            split(1, 1)
            act.wait_ge(gains_ready, 1)
            for m in range(DK):
                act.wait_ge(x_drained, 2 * m + 2)
                tail(m, m, B[0], G_FFN1[0], 0)

            for ph in PHASES:
                X, A = B[ph.swapped], B[not ph.swapped]
                lo = META if ph.last else 0
                if ph.kind == "ffn":
                    for b, (n0, t0, f0, nf) in enumerate(ph.blocks):
                        def in_group(i, first=False):
                            for j in range(4):
                                n = n0 + 4 * i + j
                                split(n + AHEAD, (j + AHEAD) % RING)
                                if first and j == 0:
                                    root(ph.s0, ph.last)
                                if j % 2 == 0:
                                    act.wait_ge(drained, n + 1)
                                    nc.scalar.activation(silu[:, lo:T], gate[:, lo:T], ACT.Silu).then_inc(silu_ready, 1)
                                else:
                                    f = 2 * i + j // 2
                                    wait_apart(act, hid_ready, t0 + f + 1)
                                    nc.scalar.activation(A[0][:, f, lo:T], hid[:, lo:T], ACT.Copy).then_inc(act_hi_ready, 1)
                        in_group(0, first=b == 0)
                        with act.Fori(1, nf // 2) as i:
                            in_group(i)
                        n1 = n0 + 2 * nf
                        final = b == len(ph.blocks) - 1

                        def out_group(i):
                            for j in range(4):
                                n = n1 + 4 * i + j
                                split(n + AHEAD, (j + AHEAD) % RING)
                                if final:
                                    wait_apart(act, drained, n + 1)
                                    tail(4 * i + j, ph.x0 + 4 * i + j, X, ph.gain, lo)
                        if final and ph.last:
                            out_group(0)
                            out_group(1)
                        else:
                            with act.Fori(0, 2) as i:
                                out_group(i)
                elif ph.kind == "attn":
                    attn_act(act, ph, split, tail, root, X, A)
                else:
                    root(ph.s0, False)
                    for m in range(DK):
                        act.wait_ge(pool_ready, m + 1)
                        nc.scalar.activation(X[0][:, m, META:T], pooled[:, META:T], ACT.Copy).then_inc(pool_hi, 1)
                    for j in range(4):
                        n = ph.n0 + j
                        split(n + AHEAD, (j + AHEAD) % RING)
                        act.wait_ge(drained, n + 1)
                        for e in range(2):
                            m = 2 * j + e
                            if e == 0:
                                act.wait_ge(pool_added, j + 1)
                            tail(m, ph.x0 + m, A, ph.gain, META)
            for m in range(DK):
                act.wait_ge(sq_ready, FINAL_X + m + 1)
                nc.scalar.activation(h[:, m, META:T], h[:, m, META:T], ACT.Copy,
                                     scale=gains[:, G_FINAL * DK + m:G_FINAL * DK + m + 1]).then_inc(scaled, 1)
            act.wait_ge(final_done, 1)
            nc.scalar.activation(sq[:, 0:4], psum[0][:, 0, 0:4], ACT.Sqrt, scale=1.0 / D,
                                 bias=eps_col[:, 0:1]).then_inc(root_ready, 1)
            for t in range(SEQ // P):
                act.wait_ge(y_scaled, 2 * t + 2)
                act.dma_start(out[0, t * P:(t + 1) * P, :], y_out[:, t, :]).then_inc(y_stored, 16)

        @block.vector
        def _(dve):
            def split(n, j):
                if isinstance(n, int) and n >= UNITS:
                    return
                dve.wait_ge(hi_ready, n + 1)
                nc.vector.tensor_tensor(w_lo[j][:, :], raw[j][:, :], w_hi[j][:, :], ALU.subtract).then_inc(lo_ready, 1)

            def tail(m, x1, xg1, X, gain, lo):
                if gain is not None:
                    dve.wait_ge(xg_hi_ready, xg1 + 1)
                    g = gains[:, gain * DK + m:gain * DK + m + 1] if isinstance(m, int) else gains[:, bass.ds(m + gain * DK, 1)]
                    nc.vector.scalar_tensor_tensor(X[1][:, m, lo:T], h[:, m, lo:T], g, X[0][:, m, lo:T],
                                                   ALU.mult, ALU.subtract).then_inc(xg_ready, 1)
                dve.wait_ge(sq_ready, x1 + 1)
                dve.wait_ge(sq_added, x1)
                nc.vector.tensor_tensor(sumsq[:, lo:T], sumsq[:, lo:T], sq[:, lo:T], ALU.add).then_inc(sq_added, 1)

            def inverse(s, last):
                dve.wait_ge(root_ready, s + 1)
                lo = META if last else 0
                nc.vector.reciprocal(rinv[:, lo:T], sq[:, lo:T]).then_inc(rinv_ready, 1)
                nc.vector.memset(sumsq[:, :], 0.0).then_inc(zeroed, 1)
                dve.wait_ge(rinv_ready, s + 1)
                dve.wait_ge(zeroed, s + 2)

            nc.vector.memset(sumsq[:, :], 0.0).then_inc(zeroed, 1)
            dve.wait_ge(zeroed, 1)
            split(0, 0)
            split(1, 1)
            dve.wait_ge(gains_t, 1)
            nc.vector.tensor_copy(gains[:, :], psum[3][:, 0, 0:8 * DK]).then_inc(gains_ready, 1)
            dve.wait_ge(gains_ready, 1)
            for m in range(DK):
                dve.wait_ge(turned, m + 1)
                nc.vector.tensor_copy(h[:, m, META:T], psum[m % 3][:, 0, :]).then_inc(x_drained, 1)
                nc.vector.tensor_copy(h[:, m, 0:META], psum[m % 3][:, 1, 0:META]).then_inc(x_drained, 1)
                dve.wait_ge(x_drained, 2 * m + 2)
                tail(m, m, m, B[0], G_FFN1[0], 0)

            for ph in PHASES:
                X, A = B[ph.swapped], B[not ph.swapped]
                lo = META if ph.last else 0
                if ph.kind == "ffn":
                    for b, (n0, t0, f0, nf) in enumerate(ph.blocks):
                        def in_group(i, first=False):
                            for j in range(4):
                                n = n0 + 4 * i + j
                                split(n + AHEAD, (j + AHEAD) % RING)
                                if first and j == 0:
                                    inverse(ph.s0, ph.last)
                                dve.wait_ge(unit_done, n + 1)
                                f = 2 * i + j // 2
                                if j % 2 == 0:
                                    nc.vector.tensor_tensor(tok(gate[:, :], ph.last), pair_of(j, ph.last),
                                                            tok(rinv[:, :], ph.last), ALU.mult).then_inc(drained, 1)
                                else:
                                    nc.vector.tensor_tensor(tok(hid[:, :], ph.last), pair_of(j, ph.last),
                                                            tok(rinv[:, :], ph.last), ALU.mult).then_inc(drained, 1)
                                    dve.wait_ge(silu_ready, t0 + f + 1)
                                    dve.wait_ge(drained, n + 1)
                                    nc.vector.tensor_tensor(hid[:, lo:T], hid[:, lo:T], silu[:, lo:T],
                                                            ALU.mult).then_inc(hid_ready, 1)
                                    dve.wait_ge(act_hi_ready, t0 + f + 1)
                                    nc.vector.tensor_tensor(A[1][:, f, lo:T], hid[:, lo:T], A[0][:, f, lo:T],
                                                            ALU.subtract).then_inc(act_ready, 1)
                        in_group(0, first=b == 0)
                        with dve.Fori(1, nf // 2) as i:
                            in_group(i)
                        n1 = n0 + 2 * nf
                        final = b == len(ph.blocks) - 1

                        def out_group(i):
                            for j in range(4):
                                n = n1 + 4 * i + j
                                m = 4 * i + j
                                split(n + AHEAD, (j + AHEAD) % RING)
                                dve.wait_ge(unit_done, n + 1)
                                hm = tok(h[:, m, :], ph.last)
                                nc.vector.scalar_tensor_tensor(hm, pair_of(j, ph.last), 0.5, hm,
                                                               ALU.mult, ALU.add).then_inc(drained, 1)
                                if final:
                                    dve.wait_ge(drained, n + 1)
                                    tail(m, ph.x0 + m, xg_base(ph) + m, X, ph.gain, lo)
                        if final and ph.last:
                            out_group(0)
                            out_group(1)
                        else:
                            with dve.Fori(0, 2) as i:
                                out_group(i)
                elif ph.kind == "attn":
                    attn_dve(dve, ph, split, tail, inverse, X, A)
                else:
                    inverse(ph.s0, False)
                    for m in range(DK):
                        c = pool_step
                        nc.vector.scalar_tensor_tensor(un, h[:, m, :], gains[:, G_MIX[1] * DK + m:G_MIX[1] * DK + m + 1],
                                                       rinv[:, :], ALU.mult, ALU.mult).then_inc(c, 1)
                        count = POOL_STEPS[m]
                        dve.wait_ge(c, count + 1)
                        src, k = un, 1
                        w = WINDOWS[m * P * len(WINDOWS) // D]
                        while k < w:
                            dst = win_a if src is not win_a else win_b
                            nc.vector.tensor_tensor(dst[:, 2 * k - 1:T], src[:, 2 * k - 1:T], src[:, k - 1:T - k],
                                                    ALU.add).then_inc(c, 1)
                            src, k, count = dst, 2 * k, count + 1
                            dve.wait_ge(c, count + 1)
                        nc.vector.scalar_tensor_tensor(pooled[:, META:T], src[:, META:T], 1.0 / w, un[:, META:T],
                                                       ALU.mult, ALU.subtract).then_inc(pool_ready, 1)
                        dve.wait_ge(pool_ready, m + 1)
                        dve.wait_ge(pool_hi, m + 1)
                        nc.vector.tensor_tensor(X[1][:, m, META:T], pooled[:, META:T], X[0][:, m, META:T],
                                                ALU.subtract).then_inc(pool_split, 1)
                    for j in range(4):
                        n = ph.n0 + j
                        split(n + AHEAD, (j + AHEAD) % RING)
                        dve.wait_ge(unit_done, n + 1)
                        for e in range(2):
                            m = 2 * j + e
                            nc.vector.scalar_tensor_tensor(
                                h[:, m, META:T], psum[j][:, e, :], gains[:, G_POOL * DK + m:G_POOL * DK + m + 1],
                                h[:, m, META:T], ALU.mult, ALU.add).then_inc(drained if e else pool_added, 1)
                        dve.wait_ge(pool_added, j + 1)
                        dve.wait_ge(drained, n + 1)
                        for e in range(2):
                            m = 2 * j + e
                            tail(m, ph.x0 + m, xg_base(ph) + m, A, ph.gain, META)
            dve.wait_ge(root_ready, len(PHASES) + 1)
            nc.vector.reciprocal(sq[:, 4:8], sq[:, 0:4]).then_inc(final_r, 1)
            dve.wait_ge(final_r, 1)
            for t in range(SEQ // P):
                for e in range(2):
                    dve.wait_ge(y_turned, 2 * t + e + 1)
                    nc.vector.tensor_scalar(y_out[:, t, e * 512:(e + 1) * 512], psum[2 + t % 2][:, e, :],
                                            sq[:, 4 + t:5 + t], None, ALU.mult).then_inc(y_scaled, 1)

        @block.tensor
        def _(pe):
            def product(n, j, nk, rhs, last, ready=None, ready0=0):
                pe.wait_ge(lo_ready, n + 1)
                if not isinstance(n, int) or n >= RING:
                    pe.wait_ge(drained, n - RING + 1)
                for k in range(nk):
                    if ready is not None:
                        pe.wait_ge(ready, ready0 + k + 1)
                    blk = slice(k * P, (k + 1) * P)
                    for w, v in ((w_hi, 0), (w_hi, 1), (w_lo, 0)):
                        for bank, c0, cols, t0 in halves(last):
                            mm = nc.tensor.matmul(psum[j][:, bank, c0:c0 + cols], w[j][:, blk],
                                                  rhs[v][:, k, t0:t0 + cols],
                                                  start=(k == 0 and w is w_hi and v == 0),
                                                  stop=(k == nk - 1 and w is w_lo))
                mm.then_inc(unit_done, 1)

            def sums(s, x1, n, last):
                pe.wait_ge(sq_added, x1)
                if n > 0:
                    pe.wait_ge(drained, n)
                for bank, c0, cols, t0 in halves(last):
                    mm = nc.tensor.matmul(psum[3][:, bank, c0:c0 + cols], ones[:, :], sumsq[:, t0:t0 + cols],
                                          start=True, stop=True)
                mm.then_inc(sums_done, 1)

            pe.wait_ge(consts, 8)
            pe.wait_ge(consts2, 1)
            pe.wait_ge(rows_landed, 80)
            nc.tensor.transpose(psum[3][:, 0, 0:8 * DK], gain_rows[:, :], ident[0:8 * DK, 0:8 * DK]).then_inc(gains_t, 1)
            pe.wait_ge(x_landed, 32)
            for m in range(DK):
                if m >= 3:
                    pe.wait_ge(x_drained, 2 * (m - 2))
                for a in range(SEQ // P):
                    nc.tensor.transpose(psum[m % 3][:, 0, a * P:(a + 1) * P], x_in[:, a, m * P:(m + 1) * P], ident[:, :])
                nc.tensor.transpose(psum[m % 3][:, 1, 0:META], meta_in[:, m * P:(m + 1) * P],
                                    ident[0:META, 0:META]).then_inc(turned, 1)
            pe.wait_ge(x_drained, 2 * DK)
            pe.wait_ge(gains_ready, 1)

            for ph in PHASES:
                X, A = B[ph.swapped], B[not ph.swapped]
                if ph.kind == "ffn":
                    for b, (n0, t0, f0, nf) in enumerate(ph.blocks):
                        def in_group(i, first=False):
                            for j in range(4):
                                n = n0 + 4 * i + j
                                if first and j == 3:
                                    pe.wait_ge(root_ready, ph.s0 + 1)
                                product(n, j, DK, X, ph.last, xg_ready if first and j == 0 else None, xg_base(ph) - DK)
                                if first and j == 0:
                                    sums(ph.s0, ph.x0, n0, ph.last)
                        in_group(0, first=b == 0)
                        with pe.Fori(1, nf // 2) as i:
                            in_group(i)
                        n1 = n0 + 2 * nf
                        with pe.Fori(0, 2) as i:
                            for j in range(4):
                                product(n1 + 4 * i + j, j, nf, A, ph.last, act_ready if j == 0 else None, t0)
                elif ph.kind == "attn":
                    attn_pe(pe, ph, product, sums, X, A)
                else:
                    sums(ph.s0, ph.x0, ph.n0, False)
                    for j in range(4):
                        pe.wait_ge(lo_ready, ph.n0 + j + 1)
                        pe.wait_ge(drained, ph.n0 + j - RING + 1)
                        if j == 3:
                            pe.wait_ge(root_ready, ph.s0 + 1)
                        pe.wait_ge(pool_split, 2 * j + 2)
                        for e in range(2):
                            for k in range(2):
                                blk = slice(k * 2 * P + e * P, k * 2 * P + (e + 1) * P)
                                for w, v in ((w_hi, 0), (w_hi, 1), (w_lo, 0)):
                                    mm = nc.tensor.matmul(psum[j][:, e, :], w[j][:, blk], X[v][:, 2 * j + k, META:T],
                                                          start=(k == 0 and w is w_hi and v == 0),
                                                          stop=(k == 1 and w is w_lo))
                        mm.then_inc(unit_done, 1)
            pe.wait_ge(drained, UNITS)
            pe.wait_ge(sq_added, FINAL_X + DK)
            for t in range(SEQ // P):
                mm = nc.tensor.matmul(psum[0][:, 0, t:t + 1], sumsq[:, META + t * P:META + (t + 1) * P], ones[:, 0:1],
                                      start=True, stop=True)
            mm.then_inc(final_done, 1)
            for t in range(SEQ // P):
                for e in range(2):
                    if t >= 2:
                        pe.wait_ge(y_scaled, 2 * (t - 2) + e + 1)
                    for a in range(4):
                        m = 4 * e + a
                        if t == 0:
                            pe.wait_ge(scaled, m + 1)
                        mm = nc.tensor.transpose(psum[2 + t % 2][:, e, a * P:(a + 1) * P],
                                                 h[:, m, META + t * P:META + (t + 1) * P], ident[:, :])
                    mm.then_inc(y_turned, 1)

        @block.gpsimd
        def _(pool):
            for t in (ident, neg_tri, causal):
                nc.gpsimd.memset(t[:, :], {id(ident): 0.0, id(neg_tri): -1.0, id(causal): 0.0}[id(t)]).then_inc(consts, 1)
            nc.gpsimd.memset(ones[:, :], 1.0).then_inc(consts, 1)
            nc.gpsimd.memset(neg_ones[:, :], -1.0).then_inc(consts, 1)
            nc.gpsimd.memset(eps_col[:, :], EPS).then_inc(consts, 1)
            nc.gpsimd.memset(qkv_scale[:, :], 1.0).then_inc(consts, 1)
            pool.wait_ge(consts, 7)
            nc.gpsimd.memset(qkv_scale[:, 0:4:3], SCALE).then_inc(consts, 1)
            nc.gpsimd.affine_select(out=ident[:, :], in_=ident[:, :], compare_op=ALU.not_equal, fill=1.0, base=0,
                                    pattern=[[-1, P]], channel_multiplier=1).then_inc(consts2, 1)
            nc.gpsimd.affine_select(out=neg_tri[:, :], in_=neg_tri[:, :], compare_op=ALU.is_ge, fill=0.0, base=0,
                                    pattern=[[-1, P]], channel_multiplier=1).then_inc(consts2, 1)
            nc.gpsimd.affine_select(out=causal[:, :], in_=causal[:, :], compare_op=ALU.is_ge, fill=MASKED, base=0,
                                    pattern=[[-1, P]], channel_multiplier=1).then_inc(consts2, 1)
            for ph in PHASES:
                if ph.kind != "attn":
                    continue
                pool.wait_ge(drained, ph.n0 + 1)
                nc.gpsimd.memset(v_tok[:, :, QT - 1, :], 0.0).then_inc(v_pad, 1)
                pool.wait_ge(fg_step, 6)
                pool.dma_start(c_dram[0], fg_sum).then_inc(c_stored, 16)
                pool.dma_start(c_dram[1], fg_neg).then_inc(c_stored, 16)
                pool.wait_ge(v_pad, 1)
                for e in range(2):
                    nc.gpsimd.memset(fx_q[e][HD:HD + 2, :], 1.0).then_inc(aug_ones, 1)
                    nc.gpsimd.memset(fx_k[e][HD:HD + 2, :], 1.0).then_inc(aug_ones, 1)
                with pool.Fori(0, 4) as hp:
                    base = 10 * hp

                    def mask(t, kn, done):
                        nc.gpsimd.affine_select(out=t[0:kn, 0:kn], in_=t[0:kn, 0:kn], compare_op=ALU.is_gt, fill=0.0,
                                                base=0, pattern=[[1, kn]], channel_multiplier=-1).then_inc(done, 1)
                    for g in range(11):
                        if g < 10:
                            wait_apart(pool, sp_done, base + g + 1)
                            mask(softplus[g % 2], key_tile(4 - g % 5)[1], sp_masked)
                        if g >= 1:
                            wait_apart(pool, w_done, base + g)
                            mask(weight[(g - 1) % 2], key_tile(4 - (g - 1) % 5)[1], w_masked)


_INS = ["x", "meta_tokens", "g_ffn1", "w_ffn1_in", "w_ffn1_out", "g_mix", "g_ffn2", "w_ffn2_in", "w_ffn2_out",
        "w_attn_in", "b_forget", "w_attn_out", "w_pool", "pool_scale", "g_final"]


def kernel(**inputs):
    import concourse.bacc as bacc
    from concourse.bass_utils import run_bass_kernel_spmd

    nc = bacc.Bacc("TRN2", target_bir_lowering=False, num_devices=1)
    arrays, args = {}, []
    for name in _INS:
        a = np.ascontiguousarray(inputs[name])
        arrays[f"in_{name}"] = a
        args.append(nc.dram_tensor(f"in_{name}", a.shape, mybir.dt.from_np(a.dtype), kind="ExternalInput").ap())
    out = nc.dram_tensor("out_y", (1, SEQ, D), F32, kind="ExternalOutput").ap()
    trunk(nc, *args, out)
    r = run_bass_kernel_spmd(nc, [arrays], core_ids=[0])
    return r.results[0]["out_y"]
```

```python
import concourse.bass as bass
from concourse import mybir
from contextlib import ExitStack
import numpy as np

F32 = mybir.dt.float32
F32R = mybir.dt.float32r
ACT = mybir.ActivationFunctionType
ALU = mybir.AluOpType
AXX = mybir.AxisListType.X

P = 128
D = 1024
DK = D // P
META = 16
SEQ = 512
T = META + SEQ
HALF = T // 2
FF = 2816
FT = FF // P
BLOCKS = [8, 8, 6]
HD = 64
NH = 8
SCALE = HD ** -0.5
WINDOWS = (2, 4, 8, 16)
EPS = 1e-6
RING = 4
UNIT = 8 * P
AHEAD = 2
QT = 5
MASKED = -3.0e38
STEPS = 8

G_FFN1, G_MIX, G_FFN2, G_FINAL, G_POOL = (0, 1), (2, 3), (4, 5), 6, 7


class Phase:
    def __init__(self, kind, n0, t0, x0, s0, xg0, gain, which, layer, last, swapped):
        self.kind, self.n0, self.t0, self.x0, self.s0, self.xg0 = kind, n0, t0, x0, s0, xg0
        self.gain, self.which, self.layer, self.last, self.swapped = gain, which, layer, last, swapped
        self.blocks = []


def plan():
    out, n, t, x, s, xg = [], 0, 0, DK, 0, DK
    order = [("ffn", 0, 0, G_MIX[0]), ("attn", 0, 0, G_FFN2[0]), ("ffn", 1, 0, G_FFN1[1]),
             ("ffn", 0, 1, None), ("pool", 0, 1, G_FFN2[1]), ("ffn", 1, 1, None)]
    swapped = False
    for at, (kind, which, layer, gain) in enumerate(order):
        ph = Phase(kind, n, t, x, s, xg, gain, which, layer, at == len(order) - 1, swapped)
        out.append(ph)
        if kind == "ffn":
            f = 0
            for nf in BLOCKS:
                ph.blocks.append((n, t, f, nf))
                n += 2 * nf + DK
                t += nf
                f += nf
        elif kind == "attn":
            n += 24 + DK
            swapped = not swapped
        else:
            n += 4
            swapped = not swapped
        x += DK
        s += 1
        xg += DK if gain is not None else 0
    return out, n


def trunk(nc, x, meta_tokens, g_ffn1, w_ffn1_in, w_ffn1_out, g_mix, g_ffn2, w_ffn2_in, w_ffn2_out,
          w_attn_in, b_forget, w_attn_out, w_pool, pool_scale, g_final, out):
    PHASES, UNITS = plan()
    w_in = (w_ffn1_in, w_ffn2_in)
    w_out = (w_ffn1_out, w_ffn2_out)
    ctx = ExitStack()
    with ctx:
        def sb(name, shape, dt=F32, at=ctx):
            return at.enter_context(nc.sbuf_tensor(name, shape, dt))

        def sem(name):
            return ctx.enter_context(nc.semaphore(name))

        h = sb("h", [P, DK, T])
        b0_hi = sb("b0_hi", [P, DK, T], F32R)
        b0_lo = sb("b0_lo", [P, DK, T], F32R)
        raw = [sb(f"raw{i}", [P, UNIT]) for i in range(RING)]
        w_hi = [sb(f"w_hi{i}", [P, UNIT], F32R) for i in range(RING)]
        w_lo = [sb(f"w_lo{i}", [P, UNIT], F32R) for i in range(RING)]
        rinv = sb("rinv", [P, T])
        sumsq = sb("sumsq", [P, T])
        gains = sb("gains", [P, 8 * DK])
        ident = sb("ident", [P, P])
        ones = sb("ones", [P, P])
        neg_tri = sb("neg_tri", [P, P])
        neg_ones = sb("neg_ones", [P, P])
        causal = sb("causal", [P, P])
        eps_col = sb("eps_col", [P, 1])
        sq = sb("sq", [P, T])
        qkv_scale = sb("qkv_scale", [P, 6])
        wf_raw = sb("wf_raw", [P, DK, NH])
        wf_hi = sb("wf_hi", [P, DK, NH], F32R)
        wf_lo = sb("wf_lo", [P, DK, NH], F32R)
        bf_col = sb("bf_col", [NH, 1])
        early = ExitStack()
        b1_hi = sb("b1_hi", [P, DK, T], F32R, early)
        b1_lo = sb("b1_lo", [P, DK, T], F32R, early)
        gate = sb("gate", [P, T], F32, early)
        silu = sb("silu", [P, T], F32, early)
        hid = sb("hid", [P, T], F32, early)
        x_in = sb("x_in", [P, SEQ // P, D], F32, early)
        meta_in = sb("meta_in", [META, D], F32, early)
        gain_rows = sb("gain_rows", [8 * DK, P], F32, early)
        y_out = x_in
        win_a = x_in[:, 0, 0:T]
        win_b = x_in[:, 1, 0:T]
        un = x_in[:, 2, 0:T]
        pooled = x_in[:, 3, 0:T]
        early.close()
        late = ExitStack()
        qkv = sb("qkv", [P, 24, T], F32, late)
        v_tok = sb("v_tok", [P, 2, QT, SEQ], F32, late)
        sb_q = [sb(f"sb_q{i}", [HD, T], F32, late) for i in range(2)]
        sb_k = [sb(f"sb_k{i}", [HD, SEQ + P], F32, late) for i in range(2)]
        fx_q = [sb(f"fx_q{i}", [HD + 2, T], F32, late) for i in range(2)]
        fx_k = [sb(f"fx_k{i}", [HD + 2, T], F32, late) for i in range(2)]
        head_v = [sb(f"head_v{i}", [P, 2, QT, HD], F32, late) for i in range(2)]
        stats = sb("stats", [P, 3, 4], F32, late)
        turned_p = [sb(f"turned_p{i}", [P, QT, P], F32, late) for i in range(2)]
        first_probs = sb("first_probs", [P, META], F32, late)
        first_turned = sb("first_turned", [META, META], F32, late)
        late.close()
        spare = [qkv[:, (8 if i < 4 else 16) + i, :] for i in range(8)]
        log1p = spare[0:2]
        softplus = spare[2:4]
        weight = spare[4:6]
        stick = spare[6]
        probs = [spare[7], sq]
        fg, fg_abs, fg_sum, fg_neg, fg_one = (t[0:NH, 0:T] for t in (sb_q[0], sb_k[0], sb_q[1], sb_k[1], fx_q[0]))
        c_dram = nc.dram_tensor("c_dram", [2, NH, T], F32).ap()
        B = ((b0_hi, b0_lo), (b1_hi, b1_lo))

        psum = [ctx.enter_context(nc.psum_tensor(f"pair{i}", [P, 2, 512], F32)) for i in range(4)]

        landed = [sem(f"landed{i}") for i in range(RING)]
        hi_ready = sem("hi_ready")
        lo_ready = sem("lo_ready")
        unit_done = sem("unit_done")
        drained = sem("drained")
        silu_ready = sem("silu_ready")
        hid_ready = sem("hid_ready")
        act_hi_ready = sem("act_hi_ready")
        act_ready = sem("act_ready")
        xg_hi_ready = sem("xg_hi_ready")
        xg_ready = sem("xg_ready")
        sq_ready = sem("sq_ready")
        sq_added = sem("sq_added")
        sums_done = sem("sums_done")
        root_ready = sem("root_ready")
        rinv_ready = sem("rinv_ready")
        x_landed = sem("x_landed")
        rows_landed = sem("rows_landed")
        consts = sem("consts")
        consts2 = sem("consts2")
        gains_t = sem("gains_t")
        gains_ready = sem("gains_ready")
        turned = sem("turned")
        x_drained = sem("x_drained")
        zeroed = sem("zeroed")
        final_done = sem("final_done")
        y_turned = sem("y_turned")
        y_scaled = sem("y_scaled")
        y_stored = sem("y_stored")
        final_r = sem("final_r")
        scaled = sem("scaled")
        pool_ready = sem("pool_ready")
        pool_hi = sem("pool_hi")
        pool_split = sem("pool_split")
        pool_step = sem("pool_step")
        pool_added = sem("pool_added")
        POOL_STEPS = [0]
        for m in range(DK):
            POOL_STEPS.append(POOL_STEPS[-1] + 1 + int(np.log2(WINDOWS[m * P * len(WINDOWS) // D])))
        FINAL_X = PHASES[-1].x0

        def xg_base(ph):
            return ph.xg0

        (fg_landed, wf_split, fg_mm, fg_step, fg_act, c_stored, vt_turned, vt_out, aug_ones,
         z_done, abs_done, exp_done, ln_done, sp_done, sp_masked, sticks_done, w_done, w_masked, sb_pv,
         s_done, s_masked, max_done, p_exp, p_inv, p_done, p_turned, pt_out, fx_pv, stick_ready,
         o_hi, o_split, v_pad) = (sem(n) for n in (
             "fg_landed wf_split fg_mm fg_step fg_act c_stored vt_turned vt_out aug_ones "
             "z_done abs_done exp_done ln_done sp_done sp_masked sticks_done w_done w_masked sb_pv "
             "s_done s_masked max_done p_exp p_inv p_done p_turned pt_out fx_pv stick_ready "
             "o_hi o_split v_pad").split())
        first_masked, first_max, first_exp, first_inv, first_p, first_zero, stick_tail = (sem(n) for n in (
            "first_masked first_max first_exp first_inv first_p first_zero stick_tail").split())
        staged = [sem(f"staged{e}") for e in range(2)]

        block = ctx.enter_context(nc.Block())

        def halves(ph_last):
            if ph_last:
                return [(0, 0, SEQ, META)]
            return [(0, 0, HALF, 0), (1, 0, HALF, HALF)]

        def pair_of(i, last=False):
            return psum[i][:, 0, :] if last else psum[i][:, :, 0:HALF]

        def tok(ap, last=False):
            return ap[:, META:T] if last else ap.rearrange("p (a b) -> p a b", a=2)

        def stick_tile(g):
            s = g % 4
            k0 = (3 - s) * P
            return k0, max(k0, META), T - max(k0, META)

        def stick_cols(g):
            return stick_tile(g)[2] + (2 * META if g % 4 == 0 else 0)

        def z_psum(g):
            return psum[0][:, g % 2, :]

        def fox_tile(g):
            return META + (g % 4) * P, 2 * META + P - META + (g % 4) * P

        def s_psum(g):
            return psum[1][:, 0, :] if g % 2 == 0 else psum[2][:, :, :].rearrange("p a b -> p (a b)")

        FIRST_S = 384
        FIRST_T = 2 * P
        o_main = psum[3]
        o_first = psum[1][:, 1, 0:2 * META].rearrange("p (a b) -> p a b", a=2)

        def count_ge(eng, sem_, count, apart=False):
            if isinstance(count, int) and count <= 0:
                return
            if apart:
                wait_apart(eng, sem_, count)
            else:
                eng.wait_ge(sem_, count)

        def steps(eng, step, drain):
            for g in range(STEPS):
                step(0, g, True)
            with eng.Fori(1, NH // 2) as hp:
                for g in range(STEPS):
                    step(hp, g, False)
            drain()

        def before(hp, g, lag, first):
            if g >= lag:
                return hp, g - lag
            return None if first else (hp - 1, g - lag + STEPS)

        def key_tile(jt):
            return jt * P, min(P, T - jt * P)

        def stage_heads(sp, ph):
            def stage(hp, e):
                rows = slice(HD * e, HD * (e + 1))
                head = 2 * hp + e

                def put(dst, src):
                    sp.dma_start(dst, src).then_inc(staged[e], 16)

                put(sb_q[e][:, :], qkv[rows, bass.ds(hp, 1), :].rearrange("p a t -> p (a t)"))
                put(sb_k[e][:, 0:T], qkv[rows, bass.ds(hp + 4, 1), :].rearrange("p a t -> p (a t)"))
                put(fx_q[e][0:HD, :], qkv[rows, bass.ds(hp + 12, 1), :].rearrange("p a t -> p (a t)"))
                put(fx_k[e][0:HD, :], qkv[rows, bass.ds(hp + 16, 1), :].rearrange("p a t -> p (a t)"))
                put(fx_q[e][HD + 1:HD + 2, :], c_dram[0, bass.ds(head, 1), :])
                put(fx_k[e][HD:HD + 1, :], c_dram[1, bass.ds(head, 1), :])
                for kind in range(2):
                    put(head_v[e][:, kind, :, :], v_tok[:, kind, :, bass.ds(head * HD, HD)])

            sp.wait_ge(drained, ph.n0 + 24)
            sp.wait_ge(vt_out, 2 * QT)
            sp.wait_ge(c_stored, 32)
            sp.wait_ge(aug_ones, 6)
            stage(0, 0)
            stage(0, 1)
            with sp.Fori(1, 4) as hp:
                for e in range(2):
                    sp.wait_ge(fx_pv, STEPS * (hp - 1) + 4 * (e + 1))
                    stage(hp, e)

        def o_tile(t, hp, kind):
            return t[:, bass.ds(hp + 4 * kind, 1), META:T].rearrange("p a t -> p (a t)")

        def o_firsts(t, hp):
            return t[:, :, :].rearrange("p (a b) t -> p a b t", a=2)[:, :, bass.ds(hp, 1), 0:META].rearrange(
                "p a b t -> p a (b t)")

        def attn_pe(pe, ph, product, sums, X, A):
            def group(i, first=False):
                for j in range(4):
                    if first and j == 3:
                        pe.wait_ge(root_ready, ph.s0 + 1)
                    if first and j == 2:
                        pe.wait_ge(fg_step, 1)
                    product(ph.n0 + 4 * i + j, j, DK, X, False, xg_ready if first and j == 0 else None, ph.xg0 - DK)
                    if first and j == 0:
                        sums(ph.s0, ph.x0, ph.n0, False)
                        pe.wait_ge(wf_split, 2)
                        for k in range(DK):
                            for w, v in ((wf_hi, 0), (wf_hi, 1), (wf_lo, 0)):
                                for e in range(2):
                                    mm = nc.tensor.matmul(psum[2][0:NH, e, 0:HALF], w[:, k, :],
                                                          X[v][:, k, e * HALF:(e + 1) * HALF],
                                                          start=(k == 0 and w is wf_hi and v == 0),
                                                          stop=(k == DK - 1 and w is wf_lo))
                        mm.then_inc(fg_mm, 1)
            group(0, True)
            with pe.Fori(1, 6) as i:
                group(i)
            pe.wait_ge(drained, ph.n0 + 24)
            for r in range(2 * QT):
                kind, jt = r // QT, r % QT
                t0, kn = key_tile(jt)
                if r >= 8:
                    pe.wait_ge(vt_out, r - 7)
                for a in range(4):
                    mm = nc.tensor.transpose(psum[r % 8 // 2][0:kn, r % 2, a * P:(a + 1) * P],
                                             qkv[:, 12 * kind + 8 + a, t0:t0 + kn], ident[:, :])
                mm.then_inc(vt_turned, 1)
            pe.wait_ge(vt_out, 2 * QT)


            def scores(hp, g):
                e, s, c = g // 4, g % 4, STEPS * hp + g
                k0, q0, nq = stick_tile(g)
                count_ge(pe, w_done, c - 1)
                if s == 0:
                    pe.wait_ge(staged[e], 128 * hp + 128)
                z = z_psum(g)
                mm = nc.tensor.matmul(z[:, 0:nq], sb_k[e][:, k0:k0 + P], sb_q[e][:, q0:T], start=True, stop=True)
                if s == 0:
                    nc.tensor.matmul(z[:, nq:nq + META], sb_k[e][:, SEQ:SEQ + P], sb_q[e][:, SEQ:T],
                                     start=False, stop=True, skip_group_check=True)
                    mm = nc.tensor.matmul(z[:, nq + META:nq + 2 * META], sb_k[e][:, 0:P], sb_q[e][:, 0:META],
                                          start=False, stop=True, skip_group_check=True)
                mm.then_inc(z_done, 1)
                q0, nk = fox_tile(g)
                count_ge(pe, pt_out, c - 1)
                sc = s_psum(g)
                for c0, c1 in ((0, min(nk, 512)), (512, nk)):
                    if c1 > c0:
                        mm = nc.tensor.matmul(sc[:, c0:c1], fx_q[e][:, q0:q0 + P], fx_k[e][:, c0:c1],
                                              start=True, stop=True)
                if s == 0:
                    mm = nc.tensor.matmul(sc[:, FIRST_S:FIRST_S + META], fx_q[e][:, 0:P], fx_k[e][:, 0:META],
                                          start=True, stop=True)
                mm.then_inc(s_done, 1)

            def turn(hp, g):
                e, s, c = g // 4, g % 4, STEPS * hp + g
                k0, q0, nq = stick_tile(g)
                z = z_psum(g)
                pe.wait_ge(sp_masked, c + 1)
                pe.wait_ge(stick_ready, c + 1)
                nc.tensor.matmul(z[:, 0:stick_cols(g)], neg_tri[:, :], softplus[g % 2][:, 0:stick_cols(g)],
                                 start=False, stop=True, skip_group_check=True)
                if s == 0:
                    later, c0 = softplus[g % 2][:, nq:nq + META], P
                else:
                    later, c0 = stick[:, k0 + P:T], k0 + P - q0
                nc.tensor.matmul(z[:, c0:nq], neg_ones[:, :], later, start=False, stop=True,
                                 skip_group_check=True).then_inc(sticks_done, 1)
                q0, nk = fox_tile(g)
                pe.wait_ge(p_done, c + 1)
                sc = s_psum(g)
                for b in range(s + 2):
                    c1 = min(b * P + P, T)
                    mm = nc.tensor.transpose(sc[0:c1 - b * P, b * P:b * P + P], probs[g % 2][:, b * P:c1], ident[:, :])
                if s == 0:
                    pe.wait_ge(first_p, 2 * hp + e + 1)
                    mm = nc.tensor.transpose(sc[0:META, FIRST_T:FIRST_T + P], first_probs[:, :], ident[:, :])
                mm.then_inc(p_turned, 1)

            def values(hp, g):
                e, s, c = g // 4, g % 4, STEPS * hp + g
                k0, q0, nq = stick_tile(g)
                rows = slice(HD * e, HD * (e + 1))
                w = weight[g % 2]
                if g == 0:
                    count_ge(pe, o_split, 3 * hp)
                pe.wait_ge(w_masked, c + 1)
                mm = nc.tensor.matmul(o_main[rows, 0, q0 - META:SEQ], head_v[e][:, 0, 3 - s, :], w[:, 0:nq],
                                      start=(s == 0), stop=True, skip_group_check=True)
                if s == 0:
                    nc.tensor.matmul(o_main[rows, 0, SEQ - META:SEQ], head_v[e][:, 0, QT - 1, :], w[:, nq:nq + META],
                                     start=False, stop=True, skip_group_check=True)
                    mm = nc.tensor.matmul(o_first[rows, 0, :], head_v[e][:, 0, 0, :], w[:, nq + META:nq + 2 * META],
                                          start=True, stop=True)
                mm.then_inc(sb_pv, 1)
                pe.wait_ge(pt_out, c + 1)
                q0, nk = fox_tile(g)
                for b in range(s + 2):
                    kb = min(P, nk - b * P)
                    mm = nc.tensor.matmul(o_main[rows, 1, q0 - META:q0 - META + P], head_v[e][0:kb, 1, b, :],
                                          turned_p[g % 2][0:kb, b, :], start=(b == 0), stop=(b == s + 1),
                                          skip_group_check=True)
                if s == 0:
                    mm = nc.tensor.matmul(o_first[rows, 1, :], head_v[e][0:META, 1, 0, :], first_turned[0:META, :],
                                          start=True, stop=True)
                mm.then_inc(fx_pv, 1)

            def pe_step(hp, g, first):
                v, t = before(hp, g, 3, first), before(hp, g, 1, first)
                if v is not None and g != 3:
                    values(*v)
                scores(hp, g)
                if t is not None:
                    turn(*t)
                if g == 3:
                    values(*v)

            def pe_drain():
                last = NH // 2 - 1
                values(last, 5)
                turn(last, 7)
                values(last, 6)
                values(last, 7)
            steps(pe, pe_step, pe_drain)
            n1 = ph.n0 + 24
            pe.wait_ge(o_split, 3 * NH // 2)
            with pe.Fori(0, 2) as i:
                for j in range(4):
                    product(n1 + 4 * i + j, j, DK, X, False)

        def attn_act(act, ph, split, tail, root, X, A):
            act.wait_ge(fg_landed, 32)
            nc.scalar.activation(wf_hi[:, :, :], wf_raw[:, :, :], ACT.Copy).then_inc(wf_split, 1)
            for j in range(4):
                split(ph.n0 + j + AHEAD, (j + AHEAD) % RING)
                if j == 0:
                    root(ph.s0, False)
            act.wait_ge(fg_step, 2)
            nc.scalar.activation(fg_abs, fg, ACT.Abs).then_inc(fg_act, 1)
            act.wait_ge(fg_act, 1)
            nc.scalar.activation(fg_abs, fg_abs, ACT.Exp, scale=-1.0).then_inc(fg_act, 1)
            act.wait_ge(fg_act, 2)
            nc.scalar.activation(fg_abs, fg_abs, ACT.Ln, bias=1.0).then_inc(fg_act, 1)
            with act.Fori(1, 6) as i:
                for j in range(4):
                    split(ph.n0 + 4 * i + j + AHEAD, (j + AHEAD) % RING)
            nc.scalar.preload_act_table_set("natural_log_exp_and_others")
            act.wait_ge(first_zero, 1)

            def act_step(hp, g, first):
                s, c = g % 4, STEPS * hp + g
                if g == 3 and not first:
                    o_upper(hp - 1)
                b = log1p[g % 2][:, 0:stick_cols(g)]
                act.wait_ge(z_done, c + 1)
                count_ge(act, sp_done, c - 1)
                nc.scalar.activation(b, z_psum(g)[:, 0:stick_cols(g)], ACT.Abs).then_inc(abs_done, 1)
                act.wait_ge(abs_done, c + 1)
                nc.scalar.activation(b, b, ACT.Exp, scale=-1.0).then_inc(exp_done, 1)
                q0, nk = fox_tile(g)
                act.wait_ge(max_done, c + 1)
                if s == 0:
                    act.wait_ge(first_max, 2 * hp + g // 4 + 1)
                count_ge(act, p_turned, c - 1)
                nc.scalar.activation(probs[g % 2][:, 0:nk], s_psum(g)[:, 0:nk], ACT.Exp, bias=stats[:, g % 2, 0:1],
                                     accum_out=stats[:, g % 2, 1:2]).then_inc(p_exp, 1)
                act.wait_ge(exp_done, c + 1)
                nc.scalar.activation(b, b, ACT.Ln, bias=1.0).then_inc(ln_done, 1)
                if s == 0:
                    nc.scalar.activation(first_probs[0:META, :], s_psum(g)[0:META, FIRST_S:FIRST_S + META], ACT.Exp,
                                         bias=stats[0:META, 2, 0:1], accum_out=stats[0:META, 2, 1:2]).then_inc(first_exp, 1)
                t = before(hp, g, 1, first)
                if t is not None:
                    stick_weight(*t)

            def stick_weight(hp, g):
                c = STEPS * hp + g
                act.wait_ge(sticks_done, c + 1)
                count_ge(act, sb_pv, c - 1)
                nc.scalar.activation(weight[g % 2][:, 0:stick_cols(g)], z_psum(g)[:, 0:stick_cols(g)],
                                     ACT.Exp).then_inc(w_done, 1)

            def o_upper(hp):
                wait_apart(act, fx_pv, STEPS * hp + STEPS)
                for kind in range(2):
                    nc.scalar.activation(o_tile(X[0], hp, kind), o_main[:, kind, :], ACT.Copy).then_inc(o_hi, 1)
                nc.scalar.activation(o_firsts(X[0], hp), o_first, ACT.Copy).then_inc(o_hi, 1)

            def act_drain():
                stick_weight(NH // 2 - 1, 7)
                o_upper(NH // 2 - 1)
            steps(act, act_step, act_drain)
            n1 = ph.n0 + 24
            with act.Fori(0, 2) as i:
                for j in range(4):
                    n = n1 + 4 * i + j
                    split(n + AHEAD, (j + AHEAD) % RING)
                    wait_apart(act, drained, n + 1)
                    tail(4 * i + j, ph.x0 + 4 * i + j, A, ph.gain, 0)

        def attn_dve(dve, ph, split, tail, inverse, X, A):
            dve.wait_ge(wf_split, 1)
            nc.vector.tensor_tensor(wf_lo[:, :, :], wf_raw[:, :, :], wf_hi[:, :, :], ALU.subtract).then_inc(wf_split, 1)

            def group(i, first=False):
                for j in range(4):
                    n = ph.n0 + 4 * i + j
                    split(n + AHEAD, (j + AHEAD) % RING)
                    if first and j == 0:
                        inverse(ph.s0, False)
                        dve.wait_ge(fg_mm, 1)
                        nc.vector.tensor_tensor(tok(fg, False), psum[2][0:NH, :, 0:HALF], tok(rinv[0:NH, :], False),
                                                ALU.mult).then_inc(fg_step, 1)
                    dve.wait_ge(unit_done, n + 1)
                    o = qkv[:, 4 * i + j, :]
                    sc = qkv_scale[:, i:i + 1] if isinstance(i, int) else qkv_scale[:, bass.ds(i, 1)]
                    nc.vector.scalar_tensor_tensor(tok(o, False), pair_of(j), sc, tok(rinv[:, :], False),
                                                   ALU.mult, ALU.mult).then_inc(drained, 1)
                    if first and j == 0:
                        dve.wait_ge(fg_step, 1)
                        nc.vector.tensor_scalar(fg, fg, bf_col[:, 0:1], None, ALU.add).then_inc(fg_step, 1)
                        nc.vector.memset(fg_one, 1.0).then_inc(fg_step, 1)
            group(0, True)
            dve.wait_ge(fg_act, 3)
            dve.wait_ge(fg_step, 3)
            nc.vector.scalar_tensor_tensor(fg, fg, 0.0, fg_abs, ALU.min, ALU.subtract).then_inc(fg_step, 1)
            dve.wait_ge(fg_step, 4)
            nc.vector.tensor_tensor_scan(fg_sum, fg_one, fg, 0.0, ALU.mult, ALU.add).then_inc(fg_step, 1)
            dve.wait_ge(fg_step, 5)
            nc.vector.tensor_scalar(fg_neg, fg_sum, -1.0, None, ALU.mult).then_inc(fg_step, 1)
            with dve.Fori(1, 6) as i:
                group(i)
            dve.wait_ge(v_pad, 1)
            for r in range(2 * QT):
                kind, jt = r // QT, r % QT
                _, kn = key_tile(jt)
                dve.wait_ge(vt_turned, r + 1)
                nc.vector.tensor_copy(v_tok[0:kn, kind, jt, :], psum[r % 8 // 2][0:kn, r % 2, :]).then_inc(vt_out, 1)

            def dve_step(hp, g, first):
                e, s, c = g // 4, g % 4, STEPS * hp + g
                if g == 3 and not first:
                    o_lower(hp - 1)
                q0, nk = fox_tile(g)
                sc = s_psum(g)
                dve.wait_ge(s_done, c + 1)
                diag = sc[:, q0:q0 + P]
                nc.vector.tensor_tensor(diag, diag, causal[:, :], ALU.add).then_inc(s_masked, 1)
                if s == 0:
                    diag = sc[0:META, FIRST_S:FIRST_S + META]
                    nc.vector.tensor_tensor(diag, diag, causal[0:META, 0:META], ALU.add).then_inc(first_masked, 1)
                dve.wait_ge(s_masked, c + 1)
                nc.vector.tensor_reduce(stats[:, g % 2, 0:1], sc[:, 0:nk], AXX, ALU.max, negate=True).then_inc(max_done, 1)
                if s == 0:
                    dve.wait_ge(first_masked, 2 * hp + e + 1)
                    nc.vector.tensor_reduce(stats[0:META, 2, 0:1], diag, AXX, ALU.max, negate=True).then_inc(first_max, 1)
                dve.wait_ge(p_exp, c + 1)
                nc.vector.reciprocal(stats[:, g % 2, 2:3], stats[:, g % 2, 1:2]).then_inc(p_inv, 1)
                w = stick_cols(g)
                dve.wait_ge(ln_done, c + 1)
                nc.vector.scalar_tensor_tensor(softplus[g % 2][:, 0:w], z_psum(g)[:, 0:w], 0.0, log1p[g % 2][:, 0:w],
                                               ALU.max, ALU.add).then_inc(sp_done, 1)
                dve.wait_ge(p_inv, c + 1)
                p = probs[g % 2][:, 0:nk]
                nc.vector.tensor_scalar(p, p, stats[:, g % 2, 2:3], None, ALU.mult).then_inc(p_done, 1)
                if s == 0:
                    dve.wait_ge(first_exp, 2 * hp + e + 1)
                    nc.vector.reciprocal(stats[0:META, 2, 2:3], stats[0:META, 2, 1:2]).then_inc(first_inv, 1)
                    dve.wait_ge(first_inv, 2 * hp + e + 1)
                    nc.vector.tensor_scalar(first_probs[0:META, :], first_probs[0:META, :], stats[0:META, 2, 2:3], None,
                                            ALU.mult).then_inc(first_p, 1)
                t = before(hp, g, 1, first)
                if t is not None:
                    fox_turned(*t)
                count_ge(dve, sticks_done, c)
                if s == 0:
                    nc.vector.memset(stick, 0.0).then_inc(stick_ready, 1)
                else:
                    _, q1, nq = stick_tile(g - 1)
                    dve.wait_ge(sp_masked, c)
                    if s == 1:
                        nc.vector.tensor_tensor(stick[:, SEQ:T], stick[:, SEQ:T], softplus[(g - 1) % 2][:, nq:nq + META],
                                                ALU.add).then_inc(stick_tail, 1)
                        dve.wait_ge(stick_tail, 2 * hp + e + 1)
                    nc.vector.tensor_tensor(stick[:, q1:T], stick[:, q1:T], softplus[(g - 1) % 2][:, 0:nq],
                                            ALU.add).then_inc(stick_ready, 1)

            def fox_turned(hp, g):
                s, c = g % 4, STEPS * hp + g
                dve.wait_ge(p_turned, c + 1)
                count_ge(dve, fx_pv, c - 1)
                src = s_psum(g)
                if s == 0:
                    nc.vector.tensor_copy(first_turned[0:META, :], src[0:META, FIRST_T:FIRST_T + META])
                if s == 3:
                    nc.vector.tensor_copy(turned_p[g % 2][0:META, 4, :], src[0:META, 4 * P:5 * P])
                full = min(s + 2, 4)
                nc.vector.tensor_copy(turned_p[g % 2][:, 0:full, :],
                                      src[:, 0:full * P].rearrange("p (b q) -> p b q", q=P)).then_inc(pt_out, 1)

            def o_lower(hp):
                for kind in range(2):
                    dve.wait_ge(o_hi, 3 * hp + kind + 1)
                    nc.vector.tensor_tensor(o_tile(X[1], hp, kind), o_main[:, kind, :], o_tile(X[0], hp, kind),
                                            ALU.subtract).then_inc(o_split, 1)
                dve.wait_ge(o_hi, 3 * hp + 3)
                nc.vector.tensor_tensor(o_firsts(X[1], hp), o_first, o_firsts(X[0], hp), ALU.subtract).then_inc(o_split, 1)

            def dve_drain():
                fox_turned(NH // 2 - 1, 7)
                o_lower(NH // 2 - 1)
            steps(dve, dve_step, dve_drain)
            n1 = ph.n0 + 24
            with dve.Fori(0, 2) as i:
                for j in range(4):
                    n = n1 + 4 * i + j
                    m = 4 * i + j
                    split(n + AHEAD, (j + AHEAD) % RING)
                    dve.wait_ge(unit_done, n + 1)
                    hm = tok(h[:, m, :])
                    nc.vector.tensor_tensor(hm, pair_of(j), hm, ALU.add).then_inc(drained, 1)
                    dve.wait_ge(drained, n + 1)
                    tail(m, ph.x0 + m, ph.xg0 + m, A, ph.gain, 0)

        def wait_apart(eng, sem_, count):
            if not isinstance(count, int):
                count = eng.to_reg(count)
            eng.wait_ge(consts, 8)
            eng.wait_ge(sem_, count)

        @block.sync
        def _(sp):
            sp.dma_start(x_in[:, :, :], x[0].rearrange("(a p) d -> p a d", p=P)).then_inc(x_landed, 16)
            sp.dma_start(meta_in[:, :], meta_tokens).then_inc(x_landed, 16)
            sp.dma_start(wf_raw[:, :, :], w_attn_in[0, :, 6 * SEQ:6 * SEQ + NH].rearrange("(k p) c -> p k c", p=P))\
              .then_inc(fg_landed, 16)
            sp.dma_start(bf_col[:, :], b_forget.rearrange("l h -> h l")).then_inc(fg_landed, 16)

            def strip(w, r0, nk, c0, width=P):
                return w[r0:r0 + nk * P, bass.ds(c0, width)].rearrange("(k p) c -> p k c", p=P)

            def dst(j, nk, width=P):
                return raw[j][:, 0:nk * width].rearrange("p (k c) -> p k c", c=width)

            def fetch_to(n, j, nk, src, width=P):
                if not isinstance(n, int) or n >= RING:
                    sp.wait_ge(lo_ready, n - RING + 1)
                sp.dma_start(dst(j, nk, width), src).then_inc(landed[j], 16)

            for ph in PHASES:
                if ph.kind == "ffn":
                    wi, wo = w_in[ph.which][ph.layer], w_out[ph.which][ph.layer]
                    for n0, t0, f0, nf in ph.blocks:
                        def in_group(i):
                            for j in range(4):
                                c = (f0 + 2 * i + j // 2) * P + (j % 2) * FF
                                fetch_to(n0 + 4 * i + j, j, DK, strip(wi, 0, DK, c))
                        in_group(0)
                        with sp.Fori(1, nf // 2) as i:
                            in_group(i)
                        with sp.Fori(0, 2) as i:
                            for j in range(4):
                                fetch_to(n0 + 2 * nf + 4 * i + j, j, nf,
                                         strip(wo, f0 * P, nf, (4 * i + j) * P))
                elif ph.kind == "attn":
                    with sp.Fori(0, 6) as i:
                        for j in range(4):
                            fetch_to(ph.n0 + 4 * i + j, j, DK, strip(w_attn_in[0], 0, DK, (4 * i + j) * P))
                    for i in range(2):
                        for j in range(4):
                            fetch_to(ph.n0 + 24 + 4 * i + j, j, DK, strip(w_attn_out[0], 0, DK, (4 * i + j) * P))
                        if i == 0:
                            stage_heads(sp, ph)
                else:
                    for j in range(4):
                        fetch_to(ph.n0 + j, j, 2, w_pool[0, j].rearrange("(k p) c -> p k c", p=P), 2 * P)
            sp.wait_ge(y_stored, 16 * (SEQ // P))

        def land_wait(eng, n, j):
            eng.wait_ge(landed[j], (n - j) * (16 // RING) + 16)

        @block.scalar
        def _(act):
            act.dma_start(gain_rows[0:16, :], g_ffn1.rearrange("l (m p) -> (l m) p", p=P)).then_inc(rows_landed, 16)
            act.dma_start(gain_rows[16:32, :], g_mix.rearrange("l (m p) -> (l m) p", p=P)).then_inc(rows_landed, 16)
            act.dma_start(gain_rows[32:48, :], g_ffn2.rearrange("l (m p) -> (l m) p", p=P)).then_inc(rows_landed, 16)
            act.dma_start(gain_rows[48:56, :], g_final.rearrange("(m p) -> m p", p=P)).then_inc(rows_landed, 16)
            act.dma_start(gain_rows[56:64, :], pool_scale.rearrange("l (m p) -> (l m) p", p=P)).then_inc(rows_landed, 16)

            def split(n, j):
                if isinstance(n, int) and n >= UNITS:
                    return
                land_wait(act, n, j)
                if not isinstance(n, int) or n >= RING:
                    act.wait_ge(unit_done, n - RING + 1)
                nc.scalar.activation(w_hi[j][:, :], raw[j][:, :], ACT.Copy).then_inc(hi_ready, 1)

            def tail(m, x1, X, gain, lo, last_sq=False):
                v = h[:, m, lo:T]
                if gain is not None:
                    nc.scalar.activation(X[0][:, m, lo:T], v, ACT.Copy,
                                         scale=gains[:, gain * DK + m:gain * DK + m + 1] if isinstance(m, int)
                                         else gains[:, bass.ds(m + gain * DK, 1)]).then_inc(xg_hi_ready, 1)
                wait_apart(act, sq_added, x1)
                nc.scalar.activation(sq[:, lo:T], v, ACT.Square).then_inc(sq_ready, 1)

            def root(s, last):
                act.wait_ge(sums_done, s + 1)
                lo = META if last else 0
                nc.scalar.activation(tok(sq[:, :], last), pair_of(3, last), ACT.Sqrt, scale=1.0 / D,
                                     bias=eps_col[:, 0:1]).then_inc(root_ready, 1)

            act.wait_ge(consts, 8)
            split(0, 0)
            split(1, 1)
            act.wait_ge(gains_ready, 1)
            for m in range(DK):
                act.wait_ge(x_drained, 2 * m + 2)
                tail(m, m, B[0], G_FFN1[0], 0)

            for ph in PHASES:
                X, A = B[ph.swapped], B[not ph.swapped]
                lo = META if ph.last else 0
                if ph.kind == "ffn":
                    for b, (n0, t0, f0, nf) in enumerate(ph.blocks):
                        def in_group(i, first=False):
                            for j in range(4):
                                n = n0 + 4 * i + j
                                split(n + AHEAD, (j + AHEAD) % RING)
                                if first and j == 0:
                                    root(ph.s0, ph.last)
                                if j % 2 == 0:
                                    act.wait_ge(drained, n + 1)
                                    nc.scalar.activation(silu[:, lo:T], gate[:, lo:T], ACT.Silu).then_inc(silu_ready, 1)
                                else:
                                    f = 2 * i + j // 2
                                    wait_apart(act, hid_ready, t0 + f + 1)
                                    nc.scalar.activation(A[0][:, f, lo:T], hid[:, lo:T], ACT.Copy).then_inc(act_hi_ready, 1)
                        in_group(0, first=b == 0)
                        with act.Fori(1, nf // 2) as i:
                            in_group(i)
                        n1 = n0 + 2 * nf
                        final = b == len(ph.blocks) - 1

                        def out_group(i):
                            for j in range(4):
                                n = n1 + 4 * i + j
                                split(n + AHEAD, (j + AHEAD) % RING)
                                if final:
                                    wait_apart(act, drained, n + 1)
                                    tail(4 * i + j, ph.x0 + 4 * i + j, X, ph.gain, lo)
                        if final and ph.last:
                            out_group(0)
                            out_group(1)
                        else:
                            with act.Fori(0, 2) as i:
                                out_group(i)
                elif ph.kind == "attn":
                    attn_act(act, ph, split, tail, root, X, A)
                else:
                    root(ph.s0, False)
                    for m in range(DK):
                        act.wait_ge(pool_ready, m + 1)
                        nc.scalar.activation(X[0][:, m, META:T], pooled[:, META:T], ACT.Copy).then_inc(pool_hi, 1)
                    for j in range(4):
                        n = ph.n0 + j
                        split(n + AHEAD, (j + AHEAD) % RING)
                        act.wait_ge(drained, n + 1)
                        for e in range(2):
                            m = 2 * j + e
                            if e == 0:
                                act.wait_ge(pool_added, j + 1)
                            tail(m, ph.x0 + m, A, ph.gain, META)
            for m in range(DK):
                act.wait_ge(sq_ready, FINAL_X + m + 1)
                nc.scalar.activation(h[:, m, META:T], h[:, m, META:T], ACT.Copy,
                                     scale=gains[:, G_FINAL * DK + m:G_FINAL * DK + m + 1]).then_inc(scaled, 1)
            act.wait_ge(final_done, 1)
            nc.scalar.activation(sq[:, 0:4], psum[0][:, 0, 0:4], ACT.Sqrt, scale=1.0 / D,
                                 bias=eps_col[:, 0:1]).then_inc(root_ready, 1)
            for t in range(SEQ // P):
                act.wait_ge(y_scaled, 2 * t + 2)
                act.dma_start(out[0, t * P:(t + 1) * P, :], y_out[:, t, :]).then_inc(y_stored, 16)

        @block.vector
        def _(dve):
            def split(n, j):
                if isinstance(n, int) and n >= UNITS:
                    return
                dve.wait_ge(hi_ready, n + 1)
                nc.vector.tensor_tensor(w_lo[j][:, :], raw[j][:, :], w_hi[j][:, :], ALU.subtract).then_inc(lo_ready, 1)

            def tail(m, x1, xg1, X, gain, lo):
                if gain is not None:
                    dve.wait_ge(xg_hi_ready, xg1 + 1)
                    g = gains[:, gain * DK + m:gain * DK + m + 1] if isinstance(m, int) else gains[:, bass.ds(m + gain * DK, 1)]
                    nc.vector.scalar_tensor_tensor(X[1][:, m, lo:T], h[:, m, lo:T], g, X[0][:, m, lo:T],
                                                   ALU.mult, ALU.subtract).then_inc(xg_ready, 1)
                dve.wait_ge(sq_ready, x1 + 1)
                dve.wait_ge(sq_added, x1)
                nc.vector.tensor_tensor(sumsq[:, lo:T], sumsq[:, lo:T], sq[:, lo:T], ALU.add).then_inc(sq_added, 1)

            def inverse(s, last):
                dve.wait_ge(root_ready, s + 1)
                lo = META if last else 0
                nc.vector.reciprocal(rinv[:, lo:T], sq[:, lo:T]).then_inc(rinv_ready, 1)
                nc.vector.memset(sumsq[:, :], 0.0).then_inc(zeroed, 1)
                dve.wait_ge(rinv_ready, s + 1)
                dve.wait_ge(zeroed, s + 2)

            nc.vector.memset(sumsq[:, :], 0.0).then_inc(zeroed, 1)
            dve.wait_ge(zeroed, 1)
            split(0, 0)
            split(1, 1)
            dve.wait_ge(gains_t, 1)
            nc.vector.tensor_copy(gains[:, :], psum[3][:, 0, 0:8 * DK]).then_inc(gains_ready, 1)
            dve.wait_ge(gains_ready, 1)
            for m in range(DK):
                dve.wait_ge(turned, m + 1)
                nc.vector.tensor_copy(h[:, m, META:T], psum[m % 3][:, 0, :]).then_inc(x_drained, 1)
                nc.vector.tensor_copy(h[:, m, 0:META], psum[m % 3][:, 1, 0:META]).then_inc(x_drained, 1)
                dve.wait_ge(x_drained, 2 * m + 2)
                tail(m, m, m, B[0], G_FFN1[0], 0)

            for ph in PHASES:
                X, A = B[ph.swapped], B[not ph.swapped]
                lo = META if ph.last else 0
                if ph.kind == "ffn":
                    for b, (n0, t0, f0, nf) in enumerate(ph.blocks):
                        def in_group(i, first=False):
                            for j in range(4):
                                n = n0 + 4 * i + j
                                split(n + AHEAD, (j + AHEAD) % RING)
                                if first and j == 0:
                                    inverse(ph.s0, ph.last)
                                dve.wait_ge(unit_done, n + 1)
                                f = 2 * i + j // 2
                                if j % 2 == 0:
                                    nc.vector.tensor_tensor(tok(gate[:, :], ph.last), pair_of(j, ph.last),
                                                            tok(rinv[:, :], ph.last), ALU.mult).then_inc(drained, 1)
                                else:
                                    nc.vector.tensor_tensor(tok(hid[:, :], ph.last), pair_of(j, ph.last),
                                                            tok(rinv[:, :], ph.last), ALU.mult).then_inc(drained, 1)
                                    dve.wait_ge(silu_ready, t0 + f + 1)
                                    dve.wait_ge(drained, n + 1)
                                    nc.vector.tensor_tensor(hid[:, lo:T], hid[:, lo:T], silu[:, lo:T],
                                                            ALU.mult).then_inc(hid_ready, 1)
                                    dve.wait_ge(act_hi_ready, t0 + f + 1)
                                    nc.vector.tensor_tensor(A[1][:, f, lo:T], hid[:, lo:T], A[0][:, f, lo:T],
                                                            ALU.subtract).then_inc(act_ready, 1)
                        in_group(0, first=b == 0)
                        with dve.Fori(1, nf // 2) as i:
                            in_group(i)
                        n1 = n0 + 2 * nf
                        final = b == len(ph.blocks) - 1

                        def out_group(i):
                            for j in range(4):
                                n = n1 + 4 * i + j
                                m = 4 * i + j
                                split(n + AHEAD, (j + AHEAD) % RING)
                                dve.wait_ge(unit_done, n + 1)
                                hm = tok(h[:, m, :], ph.last)
                                nc.vector.scalar_tensor_tensor(hm, pair_of(j, ph.last), 0.5, hm,
                                                               ALU.mult, ALU.add).then_inc(drained, 1)
                                if final:
                                    dve.wait_ge(drained, n + 1)
                                    tail(m, ph.x0 + m, xg_base(ph) + m, X, ph.gain, lo)
                        if final and ph.last:
                            out_group(0)
                            out_group(1)
                        else:
                            with dve.Fori(0, 2) as i:
                                out_group(i)
                elif ph.kind == "attn":
                    attn_dve(dve, ph, split, tail, inverse, X, A)
                else:
                    inverse(ph.s0, False)
                    for m in range(DK):
                        c = pool_step
                        nc.vector.scalar_tensor_tensor(un, h[:, m, :], gains[:, G_MIX[1] * DK + m:G_MIX[1] * DK + m + 1],
                                                       rinv[:, :], ALU.mult, ALU.mult).then_inc(c, 1)
                        count = POOL_STEPS[m]
                        dve.wait_ge(c, count + 1)
                        src, k = un, 1
                        w = WINDOWS[m * P * len(WINDOWS) // D]
                        while k < w:
                            dst = win_a if src is not win_a else win_b
                            nc.vector.tensor_tensor(dst[:, 2 * k - 1:T], src[:, 2 * k - 1:T], src[:, k - 1:T - k],
                                                    ALU.add).then_inc(c, 1)
                            src, k, count = dst, 2 * k, count + 1
                            dve.wait_ge(c, count + 1)
                        nc.vector.scalar_tensor_tensor(pooled[:, META:T], src[:, META:T], 1.0 / w, un[:, META:T],
                                                       ALU.mult, ALU.subtract).then_inc(pool_ready, 1)
                        dve.wait_ge(pool_ready, m + 1)
                        dve.wait_ge(pool_hi, m + 1)
                        nc.vector.tensor_tensor(X[1][:, m, META:T], pooled[:, META:T], X[0][:, m, META:T],
                                                ALU.subtract).then_inc(pool_split, 1)
                    for j in range(4):
                        n = ph.n0 + j
                        split(n + AHEAD, (j + AHEAD) % RING)
                        dve.wait_ge(unit_done, n + 1)
                        for e in range(2):
                            m = 2 * j + e
                            nc.vector.scalar_tensor_tensor(
                                h[:, m, META:T], psum[j][:, e, :], gains[:, G_POOL * DK + m:G_POOL * DK + m + 1],
                                h[:, m, META:T], ALU.mult, ALU.add).then_inc(drained if e else pool_added, 1)
                        dve.wait_ge(pool_added, j + 1)
                        dve.wait_ge(drained, n + 1)
                        for e in range(2):
                            m = 2 * j + e
                            tail(m, ph.x0 + m, xg_base(ph) + m, A, ph.gain, META)
            dve.wait_ge(root_ready, len(PHASES) + 1)
            nc.vector.reciprocal(sq[:, 4:8], sq[:, 0:4]).then_inc(final_r, 1)
            dve.wait_ge(final_r, 1)
            for t in range(SEQ // P):
                for e in range(2):
                    dve.wait_ge(y_turned, 2 * t + e + 1)
                    nc.vector.tensor_scalar(y_out[:, t, e * 512:(e + 1) * 512], psum[2 + t % 2][:, e, :],
                                            sq[:, 4 + t:5 + t], None, ALU.mult).then_inc(y_scaled, 1)

        @block.tensor
        def _(pe):
            def product(n, j, nk, rhs, last, ready=None, ready0=0):
                pe.wait_ge(lo_ready, n + 1)
                if not isinstance(n, int) or n >= RING:
                    pe.wait_ge(drained, n - RING + 1)
                for k in range(nk):
                    if ready is not None:
                        pe.wait_ge(ready, ready0 + k + 1)
                    blk = slice(k * P, (k + 1) * P)
                    for w, v in ((w_hi, 0), (w_hi, 1), (w_lo, 0)):
                        for bank, c0, cols, t0 in halves(last):
                            mm = nc.tensor.matmul(psum[j][:, bank, c0:c0 + cols], w[j][:, blk],
                                                  rhs[v][:, k, t0:t0 + cols],
                                                  start=(k == 0 and w is w_hi and v == 0),
                                                  stop=(k == nk - 1 and w is w_lo))
                mm.then_inc(unit_done, 1)

            def sums(s, x1, n, last):
                pe.wait_ge(sq_added, x1)
                if n > 0:
                    pe.wait_ge(drained, n)
                for bank, c0, cols, t0 in halves(last):
                    mm = nc.tensor.matmul(psum[3][:, bank, c0:c0 + cols], ones[:, :], sumsq[:, t0:t0 + cols],
                                          start=True, stop=True)
                mm.then_inc(sums_done, 1)

            pe.wait_ge(consts, 8)
            pe.wait_ge(consts2, 1)
            pe.wait_ge(rows_landed, 80)
            nc.tensor.transpose(psum[3][:, 0, 0:8 * DK], gain_rows[:, :], ident[0:8 * DK, 0:8 * DK]).then_inc(gains_t, 1)
            pe.wait_ge(x_landed, 32)
            for m in range(DK):
                if m >= 3:
                    pe.wait_ge(x_drained, 2 * (m - 2))
                for a in range(SEQ // P):
                    nc.tensor.transpose(psum[m % 3][:, 0, a * P:(a + 1) * P], x_in[:, a, m * P:(m + 1) * P], ident[:, :])
                nc.tensor.transpose(psum[m % 3][:, 1, 0:META], meta_in[:, m * P:(m + 1) * P],
                                    ident[0:META, 0:META]).then_inc(turned, 1)
            pe.wait_ge(x_drained, 2 * DK)
            pe.wait_ge(gains_ready, 1)

            for ph in PHASES:
                X, A = B[ph.swapped], B[not ph.swapped]
                if ph.kind == "ffn":
                    for b, (n0, t0, f0, nf) in enumerate(ph.blocks):
                        def in_group(i, first=False):
                            for j in range(4):
                                n = n0 + 4 * i + j
                                if first and j == 3:
                                    pe.wait_ge(root_ready, ph.s0 + 1)
                                product(n, j, DK, X, ph.last, xg_ready if first and j == 0 else None, xg_base(ph) - DK)
                                if first and j == 0:
                                    sums(ph.s0, ph.x0, n0, ph.last)
                        in_group(0, first=b == 0)
                        with pe.Fori(1, nf // 2) as i:
                            in_group(i)
                        n1 = n0 + 2 * nf
                        with pe.Fori(0, 2) as i:
                            for j in range(4):
                                product(n1 + 4 * i + j, j, nf, A, ph.last, act_ready if j == 0 else None, t0)
                elif ph.kind == "attn":
                    attn_pe(pe, ph, product, sums, X, A)
                else:
                    sums(ph.s0, ph.x0, ph.n0, False)
                    for j in range(4):
                        pe.wait_ge(lo_ready, ph.n0 + j + 1)
                        pe.wait_ge(drained, ph.n0 + j - RING + 1)
                        if j == 3:
                            pe.wait_ge(root_ready, ph.s0 + 1)
                        pe.wait_ge(pool_split, 2 * j + 2)
                        for e in range(2):
                            for k in range(2):
                                blk = slice(k * 2 * P + e * P, k * 2 * P + (e + 1) * P)
                                for w, v in ((w_hi, 0), (w_hi, 1), (w_lo, 0)):
                                    mm = nc.tensor.matmul(psum[j][:, e, :], w[j][:, blk], X[v][:, 2 * j + k, META:T],
                                                          start=(k == 0 and w is w_hi and v == 0),
                                                          stop=(k == 1 and w is w_lo))
                        mm.then_inc(unit_done, 1)
            pe.wait_ge(drained, UNITS)
            pe.wait_ge(sq_added, FINAL_X + DK)
            for t in range(SEQ // P):
                mm = nc.tensor.matmul(psum[0][:, 0, t:t + 1], sumsq[:, META + t * P:META + (t + 1) * P], ones[:, 0:1],
                                      start=True, stop=True)
            mm.then_inc(final_done, 1)
            for t in range(SEQ // P):
                for e in range(2):
                    if t >= 2:
                        pe.wait_ge(y_scaled, 2 * (t - 2) + e + 1)
                    for a in range(4):
                        m = 4 * e + a
                        if t == 0:
                            pe.wait_ge(scaled, m + 1)
                        mm = nc.tensor.transpose(psum[2 + t % 2][:, e, a * P:(a + 1) * P],
                                                 h[:, m, META + t * P:META + (t + 1) * P], ident[:, :])
                    mm.then_inc(y_turned, 1)

        @block.gpsimd
        def _(pool):
            for t in (ident, neg_tri, causal):
                nc.gpsimd.memset(t[:, :], {id(ident): 0.0, id(neg_tri): -1.0, id(causal): 0.0}[id(t)]).then_inc(consts, 1)
            nc.gpsimd.memset(ones[:, :], 1.0).then_inc(consts, 1)
            nc.gpsimd.memset(neg_ones[:, :], -1.0).then_inc(consts, 1)
            nc.gpsimd.memset(eps_col[:, :], EPS).then_inc(consts, 1)
            nc.gpsimd.memset(qkv_scale[:, :], 1.0).then_inc(consts, 1)
            pool.wait_ge(consts, 7)
            nc.gpsimd.memset(qkv_scale[:, 0:4:3], SCALE).then_inc(consts, 1)
            nc.gpsimd.affine_select(out=ident[:, :], in_=ident[:, :], compare_op=ALU.not_equal, fill=1.0, base=0,
                                    pattern=[[-1, P]], channel_multiplier=1).then_inc(consts2, 1)
            nc.gpsimd.affine_select(out=neg_tri[:, :], in_=neg_tri[:, :], compare_op=ALU.is_ge, fill=0.0, base=0,
                                    pattern=[[-1, P]], channel_multiplier=1).then_inc(consts2, 1)
            nc.gpsimd.affine_select(out=causal[:, :], in_=causal[:, :], compare_op=ALU.is_ge, fill=MASKED, base=0,
                                    pattern=[[-1, P]], channel_multiplier=1).then_inc(consts2, 1)
            for ph in PHASES:
                if ph.kind != "attn":
                    continue
                pool.wait_ge(drained, ph.n0 + 1)
                nc.gpsimd.memset(v_tok[:, :, QT - 1, :], 0.0).then_inc(v_pad, 1)
                pool.wait_ge(fg_step, 6)
                pool.dma_start(c_dram[0], fg_sum).then_inc(c_stored, 16)
                pool.dma_start(c_dram[1], fg_neg).then_inc(c_stored, 16)
                pool.wait_ge(v_pad, 1)
                for e in range(2):
                    nc.gpsimd.memset(fx_q[e][HD:HD + 2, :], 1.0).then_inc(aug_ones, 1)
                    nc.gpsimd.memset(fx_k[e][HD:HD + 2, :], 1.0).then_inc(aug_ones, 1)
                pool.wait_ge(aug_ones, 4)
                for e in range(2):
                    nc.gpsimd.memset(sb_k[e][:, T:SEQ + P], 0.0).then_inc(aug_ones, 1)
                nc.gpsimd.memset(first_probs[:, :], 0.0).then_inc(first_zero, 1)

                def mask(t, g, done):
                    _, q0, nq = stick_tile(g)
                    if g % 4 == 0:
                        both = t[:, nq:nq + 2 * META].rearrange("p (a b) -> p a b", a=2)
                        nc.gpsimd.affine_select(out=both, in_=both, compare_op=ALU.is_gt, fill=0.0, base=0,
                                                pattern=[[0, 2], [1, META]], channel_multiplier=-1)
                    ahead = META if g % 4 == 3 else 0
                    own = t[:, 0:P - ahead]
                    nc.gpsimd.affine_select(out=own, in_=own, compare_op=ALU.is_gt, fill=0.0, base=ahead,
                                            pattern=[[1, P - ahead]], channel_multiplier=-1).then_inc(done, 1)

                def weight_mask(hp, g):
                    wait_apart(pool, w_done, STEPS * hp + g + 1)
                    mask(weight[g % 2], g, w_masked)

                def pool_step_(hp, g, first):
                    wait_apart(pool, sp_done, STEPS * hp + g + 1)
                    mask(softplus[g % 2], g, sp_masked)
                    t = before(hp, g, 1, first)
                    if t is not None:
                        weight_mask(*t)
                steps(pool, pool_step_, lambda: weight_mask(NH // 2 - 1, 7))


_INS = ["x", "meta_tokens", "g_ffn1", "w_ffn1_in", "w_ffn1_out", "g_mix", "g_ffn2", "w_ffn2_in", "w_ffn2_out",
        "w_attn_in", "b_forget", "w_attn_out", "w_pool", "pool_scale", "g_final"]


def kernel(**inputs):
    import concourse.bacc as bacc
    from concourse.bass_utils import run_bass_kernel_spmd

    nc = bacc.Bacc("TRN2", target_bir_lowering=False, num_devices=1)
    arrays, args = {}, []
    for name in _INS:
        a = np.ascontiguousarray(inputs[name])
        arrays[f"in_{name}"] = a
        args.append(nc.dram_tensor(f"in_{name}", a.shape, mybir.dt.from_np(a.dtype), kind="ExternalInput").ap())
    out = nc.dram_tensor("out_y", (1, SEQ, D), F32, kind="ExternalOutput").ap()
    trunk(nc, *args, out)
    r = run_bass_kernel_spmd(nc, [arrays], core_ids=[0])
    return r.results[0]["out_y"]
```

```python
import concourse.bass as bass
from concourse import mybir
from contextlib import ExitStack
import numpy as np

F32 = mybir.dt.float32
F32R = mybir.dt.float32r
ACT = mybir.ActivationFunctionType
ALU = mybir.AluOpType
AXX = mybir.AxisListType.X

P = 128
D = 1024
DK = D // P
META = 16
SEQ = 512
T = META + SEQ
HALF = T // 2
FF = 2816
FT = FF // P
BLOCKS = [8, 8, 6]
HD = 64
NH = 8
SCALE = HD ** -0.5
WINDOWS = (2, 4, 8, 16)
EPS = 1e-6
RING = 4
UNIT = 8 * P
AHEAD = 2
QT = 5
MASKED = -3.0e38
BAND = P + max(WINDOWS) - 1
STEPS = 8

G_FFN1, G_MIX, G_FFN2, G_FINAL, G_POOL = (0, 1), (2, 3), (4, 5), 6, 7


class Phase:
    def __init__(self, kind, n0, t0, x0, s0, xg0, gain, which, layer, last, swapped):
        self.kind, self.n0, self.t0, self.x0, self.s0, self.xg0 = kind, n0, t0, x0, s0, xg0
        self.gain, self.which, self.layer, self.last, self.swapped = gain, which, layer, last, swapped
        self.blocks = []


def plan():
    out, n, t, x, s, xg = [], 0, 0, DK, 0, DK
    order = [("ffn", 0, 0, G_MIX[0]), ("attn", 0, 0, G_FFN2[0]), ("ffn", 1, 0, G_FFN1[1]),
             ("ffn", 0, 1, G_MIX[1]), ("pool", 0, 1, G_FFN2[1]), ("ffn", 1, 1, None)]
    swapped = False
    for at, (kind, which, layer, gain) in enumerate(order):
        ph = Phase(kind, n, t, x, s, xg, gain, which, layer, at == len(order) - 1, swapped)
        out.append(ph)
        if kind == "ffn":
            f = 0
            for nf in BLOCKS:
                ph.blocks.append((n, t, f, nf))
                n += 2 * nf + DK
                t += nf
                f += nf
        elif kind == "attn":
            n += 24 + DK
            swapped = not swapped
        else:
            n += 4
            swapped = not swapped
        x += DK
        s += 1
        xg += DK if gain is not None else 0
    return out, n


def trunk(nc, x, meta_tokens, g_ffn1, w_ffn1_in, w_ffn1_out, g_mix, g_ffn2, w_ffn2_in, w_ffn2_out,
          w_attn_in, b_forget, w_attn_out, w_pool, pool_scale, g_final, out):
    PHASES, UNITS = plan()
    w_in = (w_ffn1_in, w_ffn2_in)
    w_out = (w_ffn1_out, w_ffn2_out)
    ctx = ExitStack()
    with ctx:
        def sb(name, shape, dt=F32, at=ctx):
            return at.enter_context(nc.sbuf_tensor(name, shape, dt))

        def sem(name):
            return ctx.enter_context(nc.semaphore(name))

        h = sb("h", [P, DK, T])
        b0_hi = sb("b0_hi", [P, DK, T], F32R)
        b0_lo = sb("b0_lo", [P, DK, T], F32R)
        raw = [sb(f"raw{i}", [P, UNIT]) for i in range(RING)]
        w_hi = [sb(f"w_hi{i}", [P, UNIT], F32R) for i in range(RING)]
        w_lo = [sb(f"w_lo{i}", [P, UNIT], F32R) for i in range(RING)]
        rinv = sb("rinv", [P, T])
        sumsq = sb("sumsq", [P, T])
        gains = sb("gains", [P, 8 * DK])
        ident = sb("ident", [P, P])
        ones = sb("ones", [P, P])
        neg_tri = sb("neg_tri", [P, P])
        neg_ones = sb("neg_ones", [P, P])
        causal = sb("causal", [P, P])
        eps_col = sb("eps_col", [P, 1])
        root_col = sb("root_col", [P, 8])
        rinv_col = sb("rinv_col", [P, 8])
        sq = sb("sq", [P, T])
        qkv_scale = sb("qkv_scale", [P, 6])
        wf_raw = sb("wf_raw", [P, DK, NH])
        wf_hi = sb("wf_hi", [P, DK, NH], F32R)
        wf_lo = sb("wf_lo", [P, DK, NH], F32R)
        bf_col = sb("bf_col", [NH, 1])
        early = ExitStack()
        b1_hi = sb("b1_hi", [P, DK, T], F32R, early)
        b1_lo = sb("b1_lo", [P, DK, T], F32R, early)
        gate = sb("gate", [P, T], F32, early)
        silu = sb("silu", [P, T], F32, early)
        hid = sb("hid", [P, T], F32, early)
        x_in = sb("x_in", [P, SEQ // P, D], F32, early)
        meta_in = sb("meta_in", [META, D], F32, early)
        first_rows = sb("first_rows", [2 * DK, P], F32, early)
        gain_rows = sb("gain_rows", [6 * DK, P], F32, early)
        y_out = x_in
        z_tok = sb("z_tok", [P, QT, D], F32, early)
        band = sb("band", [P, len(WINDOWS), BAND], F32, early)
        y_gained = z_tok[:, :, :].rearrange("p a c -> p (a c)")
        early.close()
        late = ExitStack()
        qkv = sb("qkv", [P, 24, T], F32, late)
        v_tok = sb("v_tok", [P, 2, QT, SEQ], F32, late)
        sb_q = [sb(f"sb_q{i}", [HD, T], F32, late) for i in range(2)]
        sb_k = [sb(f"sb_k{i}", [HD, SEQ + P], F32, late) for i in range(2)]
        fx_q = [sb(f"fx_q{i}", [HD + 2, T], F32, late) for i in range(2)]
        fx_k = [sb(f"fx_k{i}", [HD + 2, T], F32, late) for i in range(2)]
        head_v = [sb(f"head_v{i}", [P, 2, QT, HD], F32, late) for i in range(2)]
        stats = sb("stats", [P, 3, 4], F32, late)
        turned_p = [sb(f"turned_p{i}", [P, QT, P], F32, late) for i in range(2)]
        first_probs = sb("first_probs", [P, META], F32, late)
        first_turned = sb("first_turned", [META, META], F32, late)
        late.close()
        spare = [qkv[:, (8 if i < 4 else 16) + i, :] for i in range(8)]
        log1p = spare[0:2]
        softplus = spare[2:4]
        weight = spare[4:6]
        stick = spare[6]
        probs = [sq, spare[7]]
        fg, fg_abs, fg_sum, fg_neg, fg_one = (t[0:NH, 0:T] for t in (sb_q[0], sb_k[0], sb_q[1], sb_k[1], fx_q[0]))
        c_dram = nc.dram_tensor("c_dram", [2, NH, T], F32).ap()
        B = ((b0_hi, b0_lo), (b1_hi, b1_lo))

        psum = [ctx.enter_context(nc.psum_tensor(f"pair{i}", [P, 2, 512], F32)) for i in range(4)]

        landed = [sem(f"landed{i}") for i in range(RING)]
        hi_ready = sem("hi_ready")
        lo_ready = sem("lo_ready")
        unit_done = sem("unit_done")
        drained = sem("drained")
        silu_ready = sem("silu_ready")
        hid_ready = sem("hid_ready")
        act_hi_ready = sem("act_hi_ready")
        act_ready = sem("act_ready")
        xg_hi_ready = sem("xg_hi_ready")
        xg_ready = sem("xg_ready")
        sq_ready = sem("sq_ready")
        sq_added = sem("sq_added")
        sums_done = sem("sums_done")
        root_ready = sem("root_ready")
        rinv_ready = sem("rinv_ready")
        x_landed = [sem(f"x_landed{i}") for i in range(4)]
        meta_landed = sem("meta_landed")
        meta_turned = sem("meta_turned")
        meta_drained = sem("meta_drained")
        first_landed = sem("first_landed")
        rows_landed = sem("rows_landed")
        consts = sem("consts")
        consts2 = sem("consts2")
        gains_t = sem("gains_t")
        gains_ready = sem("gains_ready")
        turned = sem("turned")
        x_drained = sem("x_drained")
        zeroed = sem("zeroed")
        y_turned = sem("y_turned")
        y_apart = sem("y_apart")
        y_first = sem("y_first")
        y_second = sem("y_second")
        y_stored = sem("y_stored")
        scaled = sem("scaled")
        bands = sem("bands")
        z_turned = sem("z_turned")
        z_first = sem("z_first")
        z_second = sem("z_second")
        pool_done = sem("pool_done")
        pool_added = sem("pool_added")
        FINAL_X = PHASES[-1].x0

        def xg_base(ph):
            return ph.xg0

        (fg_landed, wf_split, fg_mm, fg_step, fg_act, c_stored, vt_turned, vt_even, vt_odd, aug_ones,
         z_done, abs_done, exp_done, ln_done, sp_done, sp_masked, sticks_done, w_done, w_masked, sb_pv,
         s_done, s_masked, max_done, p_exp, p_inv, p_done, p_turned, pt_out, fx_pv, stick_ready,
         o_hi, o_split, v_pad) = (sem(n) for n in (
             "fg_landed wf_split fg_mm fg_step fg_act c_stored vt_turned vt_even vt_odd aug_ones "
             "z_done abs_done exp_done ln_done sp_done sp_masked sticks_done w_done w_masked sb_pv "
             "s_done s_masked max_done p_exp p_inv p_done p_turned pt_out fx_pv stick_ready "
             "o_hi o_split v_pad").split())
        first_masked, first_max, first_exp, first_inv, first_p, first_zero, stick_tail = (sem(n) for n in (
            "first_masked first_max first_exp first_inv first_p first_zero stick_tail").split())
        staged = [sem(f"staged{e}") for e in range(2)]
        staged_v = [sem(f"staged_v{e}") for e in range(2)]

        block = ctx.enter_context(nc.Block())

        def halves(ph_last):
            if ph_last:
                return [(0, 0, SEQ, META)]
            return [(0, 0, HALF, 0), (1, 0, HALF, HALF)]

        def pair_of(i, last=False):
            return psum[i][:, 0, :] if last else psum[i][:, :, 0:HALF]

        def tok(ap, last=False):
            return ap[:, META:T] if last else ap.rearrange("p (a b) -> p a b", a=2)

        def stick_tile(g):
            s = g % 4
            k0 = (3 - s) * P
            return k0, max(k0, META), T - max(k0, META)

        def stick_cols(g):
            return stick_tile(g)[2] + (2 * META if g % 4 == 0 else 0)

        def z_psum(g):
            return psum[0][:, g % 2, :]

        def fox_tile(g):
            return META + (g % 4) * P, 2 * META + P - META + (g % 4) * P

        def s_psum(g):
            return psum[1][:, 0, :] if g % 2 == 0 else psum[2][:, :, :].rearrange("p a b -> p (a b)")

        FIRST_S = 384
        FIRST_T = 2 * P
        o_main = psum[3]
        o_first = psum[1][:, 1, 0:2 * META].rearrange("p (a b) -> p a b", a=2)

        def count_ge(eng, sem_, count, apart=False):
            if isinstance(count, int) and count <= 0:
                return
            if apart:
                wait_apart(eng, sem_, count)
            else:
                eng.wait_ge(sem_, count)

        def steps(eng, step, drain):
            for g in range(STEPS):
                step(0, g, True)
            with eng.Fori(1, NH // 2) as hp:
                for g in range(STEPS):
                    step(hp, g, False)
            drain()

        def before(hp, g, lag, first):
            if g >= lag:
                return hp, g - lag
            return None if first else (hp - 1, g - lag + STEPS)

        def v_bank(r):
            bank = r + 3 if r < QT else 6 + (r + 1) % 2
            return psum[bank // 2][:, bank % 2, :]

        def v_turned_out(eng, r, copy):
            kind, jt = r // QT, r % QT
            _, kn = key_tile(jt)
            eng.wait_ge(vt_turned, r + 1)
            if jt == QT - 1:
                eng.wait_ge(v_pad, 1)
            copy(v_tok[0:kn, kind, jt, :], v_bank(r)[0:kn, :]).then_inc(vt_odd if r % 2 else vt_even, 1)

        def key_tile(jt):
            return jt * P, min(P, T - jt * P)

        def stage_heads(sp, ph):
            def stage_qk(hp, e):
                rows = slice(HD * e, HD * (e + 1))
                head = 2 * hp + e

                def put(dst, src):
                    sp.dma_start(dst, src).then_inc(staged[e], 16)

                put(sb_q[e][:, :], qkv[rows, bass.ds(hp, 1), :].rearrange("p a t -> p (a t)"))
                put(sb_k[e][:, 0:T], qkv[rows, bass.ds(hp + 4, 1), :].rearrange("p a t -> p (a t)"))
                put(fx_q[e][0:HD, :], qkv[rows, bass.ds(hp + 12, 1), :].rearrange("p a t -> p (a t)"))
                put(fx_k[e][0:HD, :], qkv[rows, bass.ds(hp + 16, 1), :].rearrange("p a t -> p (a t)"))
                put(fx_q[e][HD + 1:HD + 2, :], c_dram[0, bass.ds(head, 1), :])
                put(fx_k[e][HD:HD + 1, :], c_dram[1, bass.ds(head, 1), :])

            def stage_v(hp, e):
                for kind in range(2):
                    sp.dma_start(head_v[e][:, kind, :, :],
                                 v_tok[:, kind, :, bass.ds((2 * hp + e) * HD, HD)]).then_inc(staged_v[e], 16)

            sp.wait_ge(drained, ph.n0 + 20)
            sp.wait_ge(c_stored, 32)
            sp.wait_ge(aug_ones, 6)
            stage_qk(0, 0)
            stage_qk(0, 1)
            sp.wait_ge(vt_even, QT)
            sp.wait_ge(vt_odd, QT)
            stage_v(0, 0)
            stage_v(0, 1)
            with sp.Fori(1, 4) as hp:
                for e in range(2):
                    sp.wait_ge(s_done, STEPS * (hp - 1) + 4 * (e + 1))
                    stage_qk(hp, e)
                    sp.wait_ge(fx_pv, STEPS * (hp - 1) + 4 * (e + 1))
                    stage_v(hp, e)

        def o_tile(t, hp, kind):
            return t[:, bass.ds(hp + 4 * kind, 1), META:T].rearrange("p a t -> p (a t)")

        def o_firsts(t, hp):
            return t[:, :, :].rearrange("p (a b) t -> p a b t", a=2)[:, :, bass.ds(hp, 1), 0:META].rearrange(
                "p a b t -> p a (b t)")

        def attn_pe(pe, ph, product, sums, X, A):
            def group(i, first=False):
                for j in range(4):
                    if first and j == 3:
                        pe.wait_ge(root_ready, ph.s0 + 1)
                    if first and j == 2:
                        pe.wait_ge(fg_step, 1)
                    product(ph.n0 + 4 * i + j, j, DK, X, False, xg_ready if first and j == 0 else None, ph.xg0 - DK)
                    if first and j == 0:
                        sums(ph.s0, ph.x0, ph.n0, False)
                        pe.wait_ge(wf_split, 2)
                        for k in range(DK):
                            for w, v in ((wf_hi, 0), (wf_hi, 1), (wf_lo, 0)):
                                for e in range(2):
                                    mm = nc.tensor.matmul(psum[2][0:NH, e, 0:HALF], w[:, k, :],
                                                          X[v][:, k, e * HALF:(e + 1) * HALF],
                                                          start=(k == 0 and w is wf_hi and v == 0),
                                                          stop=(k == DK - 1 and w is wf_lo))
                        mm.then_inc(fg_mm, 1)
            group(0, True)
            with pe.Fori(1, 6) as i:
                group(i)
            def turn_v(r):
                kind, jt = r // QT, r % QT
                t0, kn = key_tile(jt)
                if r < 4:
                    pe.wait_ge(drained, ph.n0 + 22 + (r + 1) // 2)
                elif r >= QT:
                    pe.wait_ge(vt_odd if r % 2 else vt_even, (r - 2) // 2 + 1)
                for a in range(4):
                    mm = nc.tensor.transpose(v_bank(r)[0:kn, a * P:(a + 1) * P],
                                             qkv[:, 12 * kind + 8 + a, t0:t0 + kn], ident[:, :])
                mm.then_inc(vt_turned, 1)

            for r in range(QT):
                turn_v(r)

            def scores(hp, g):
                e, s, c = g // 4, g % 4, STEPS * hp + g
                k0, q0, nq = stick_tile(g)
                count_ge(pe, w_done, c - 1)
                if s == 0:
                    pe.wait_ge(staged[e], 96 * hp + 96)
                z = z_psum(g)
                mm = nc.tensor.matmul(z[:, 0:nq], sb_k[e][:, k0:k0 + P], sb_q[e][:, q0:T], start=True, stop=True)
                if s == 0:
                    nc.tensor.matmul(z[:, nq:nq + META], sb_k[e][:, SEQ:SEQ + P], sb_q[e][:, SEQ:T],
                                     start=False, stop=True, skip_group_check=True)
                    mm = nc.tensor.matmul(z[:, nq + META:nq + 2 * META], sb_k[e][:, 0:P], sb_q[e][:, 0:META],
                                          start=False, stop=True, skip_group_check=True)
                mm.then_inc(z_done, 1)
                q0, nk = fox_tile(g)
                count_ge(pe, pt_out, c - 1)
                sc = s_psum(g)
                for c0, c1 in ((0, min(nk, 512)), (512, nk)):
                    if c1 > c0:
                        mm = nc.tensor.matmul(sc[:, c0:c1], fx_q[e][:, q0:q0 + P], fx_k[e][:, c0:c1],
                                              start=True, stop=True)
                if s == 0:
                    mm = nc.tensor.matmul(sc[:, FIRST_S:FIRST_S + META], fx_q[e][:, 0:P], fx_k[e][:, 0:META],
                                          start=True, stop=True)
                mm.then_inc(s_done, 1)

            def sticks(hp, g):
                e, s, c = g // 4, g % 4, STEPS * hp + g
                k0, q0, nq = stick_tile(g)
                z = z_psum(g)
                pe.wait_ge(sp_masked, c + 1)
                if s > 0:
                    pe.wait_ge(stick_ready, c + 1)
                nc.tensor.matmul(z[:, 0:stick_cols(g)], neg_tri[:, :], softplus[g % 2][:, 0:stick_cols(g)],
                                 start=False, stop=True, skip_group_check=True)
                if s == 0:
                    later, c0 = softplus[g % 2][:, nq:nq + META], P
                else:
                    later, c0 = stick[:, k0 + P:T], k0 + P - q0
                nc.tensor.matmul(z[:, c0:nq], neg_ones[:, :], later, start=False, stop=True,
                                 skip_group_check=True).then_inc(sticks_done, 1)

            def turn(hp, g):
                e, s, c = g // 4, g % 4, STEPS * hp + g
                q0, nk = fox_tile(g)
                pe.wait_ge(p_done, c + 1)
                if s == 0:
                    pe.wait_ge(first_exp, 2 * hp + e + 1)
                sc = s_psum(g)
                for b in range(s + 2):
                    c1 = min(b * P + P, T)
                    mm = nc.tensor.transpose(sc[0:c1 - b * P, b * P:b * P + P], probs[g % 2][:, b * P:c1], ident[:, :])
                if s == 0:
                    pe.wait_ge(first_p, 2 * hp + e + 1)
                    mm = nc.tensor.transpose(sc[0:META, FIRST_T:FIRST_T + P], first_probs[:, :], ident[:, :])
                mm.then_inc(p_turned, 1)

            def values(hp, g):
                e, s, c = g // 4, g % 4, STEPS * hp + g
                k0, q0, nq = stick_tile(g)
                rows = slice(HD * e, HD * (e + 1))
                w = weight[g % 2]
                if g == 0:
                    count_ge(pe, o_split, 3 * hp)
                if s == 0:
                    pe.wait_ge(staged_v[e], 32 * hp + 32)
                pe.wait_ge(w_masked, c + 1)
                mm = nc.tensor.matmul(o_main[rows, 0, q0 - META:SEQ], head_v[e][:, 0, 3 - s, :], w[:, 0:nq],
                                      start=(s == 0), stop=True, skip_group_check=True)
                if s == 0:
                    nc.tensor.matmul(o_main[rows, 0, SEQ - META:SEQ], head_v[e][:, 0, QT - 1, :], w[:, nq:nq + META],
                                     start=False, stop=True, skip_group_check=True)
                    mm = nc.tensor.matmul(o_first[rows, 0, :], head_v[e][:, 0, 0, :], w[:, nq + META:nq + 2 * META],
                                          start=True, stop=True)
                mm.then_inc(sb_pv, 1)
                pe.wait_ge(pt_out, c + 1)
                q0, nk = fox_tile(g)
                for b in range(s + 2):
                    kb = min(P, nk - b * P)
                    mm = nc.tensor.matmul(o_main[rows, 1, q0 - META:q0 - META + P], head_v[e][0:kb, 1, b, :],
                                          turned_p[g % 2][0:kb, b, :], start=(b == 0), stop=(b == s + 1),
                                          skip_group_check=True)
                if s == 0:
                    mm = nc.tensor.matmul(o_first[rows, 1, :], head_v[e][0:META, 1, 0, :], first_turned[0:META, :],
                                          start=True, stop=True)
                mm.then_inc(fx_pv, 1)

            def pe_step(hp, g, first):
                v, t = before(hp, g, 3, first), before(hp, g, 1, first)
                if first and g == 1:
                    for r in range(QT, 2 * QT):
                        turn_v(r)
                    pe.wait_ge(vt_odd, 1)
                    pe.wait_ge(vt_even, 2)
                scores(hp, g)
                if v is not None and g != 3:
                    values(*v)
                if t is not None:
                    sticks(*t)
                    turn(*t)
                if g == 3:
                    if first:
                        pe.wait_ge(vt_even, QT)
                        pe.wait_ge(vt_odd, QT)
                    values(*v)

            def pe_drain():
                last = NH // 2 - 1
                values(last, 5)
                sticks(last, 7)
                turn(last, 7)
                values(last, 6)
                values(last, 7)
            steps(pe, pe_step, pe_drain)
            n1 = ph.n0 + 24
            pe.wait_ge(o_split, 3 * NH // 2)
            with pe.Fori(0, 2) as i:
                for j in range(4):
                    product(n1 + 4 * i + j, j, DK, X, False)

        def attn_act(act, ph, split, tail, root, X, A):
            act.wait_ge(fg_landed, 32)
            nc.scalar.activation(wf_hi[:, :, :], wf_raw[:, :, :], ACT.Copy).then_inc(wf_split, 1)
            for j in range(4):
                for ahead in splits_of(True, j):
                    split(ph.n0 + j + ahead, (j + ahead) % RING)
                if j == 0:
                    root(ph.s0, False)
            act.wait_ge(fg_step, 2)
            nc.scalar.activation(fg_abs, fg, ACT.Abs).then_inc(fg_act, 1)
            act.wait_ge(fg_act, 1)
            nc.scalar.activation(fg_abs, fg_abs, ACT.Exp, scale=-1.0).then_inc(fg_act, 1)
            act.wait_ge(fg_act, 2)
            nc.scalar.activation(fg_abs, fg_abs, ACT.Ln, bias=1.0).then_inc(fg_act, 1)
            with act.Fori(1, 6) as i:
                for j in range(4):
                    split(ph.n0 + 4 * i + j + AHEAD, (j + AHEAD) % RING)
            nc.scalar.preload_act_table_set("natural_log_exp_and_others")
            act.wait_ge(first_zero, 1)

            def copy(dst, src):
                return nc.scalar.activation(dst, src, ACT.Copy)

            for r in range(1, QT, 2):
                v_turned_out(act, r, copy)

            def act_step(hp, g, first):
                s, c = g % 4, STEPS * hp + g
                if g == 3 and not first:
                    o_upper(hp - 1)
                b = log1p[g % 2][:, 0:stick_cols(g)]
                act.wait_ge(z_done, c + 1)
                count_ge(act, sp_done, c - 1)
                nc.scalar.activation(b, z_psum(g)[:, 0:stick_cols(g)], ACT.Abs).then_inc(abs_done, 1)
                act.wait_ge(abs_done, c + 1)
                nc.scalar.activation(b, b, ACT.Exp, scale=-1.0).then_inc(exp_done, 1)
                act.wait_ge(exp_done, c + 1)
                nc.scalar.activation(b, b, ACT.Ln, bias=1.0).then_inc(ln_done, 1)
                t = before(hp, g, 1, first)
                if t is not None:
                    stick_weight(*t)
                q0, nk = fox_tile(g)
                act.wait_ge(max_done, c + 1)
                if s == 0:
                    act.wait_ge(first_max, 2 * hp + g // 4 + 1)
                count_ge(act, p_turned, c - 1)
                nc.scalar.activation(probs[g % 2][:, 0:nk], s_psum(g)[:, 0:nk], ACT.Exp, bias=stats[:, g % 2, 0:1],
                                     accum_out=stats[:, g % 2, 1:2]).then_inc(p_exp, 1)
                if s == 0:
                    nc.scalar.activation(first_probs[0:META, :], s_psum(g)[0:META, FIRST_S:FIRST_S + META], ACT.Exp,
                                         bias=stats[0:META, 2, 0:1], accum_out=stats[0:META, 2, 1:2]).then_inc(first_exp, 1)
                if first and g == 0:
                    for r in range(QT, 2 * QT, 2):
                        v_turned_out(act, r, copy)

            def stick_weight(hp, g):
                c = STEPS * hp + g
                act.wait_ge(sticks_done, c + 1)
                count_ge(act, sb_pv, c - 1)
                nc.scalar.activation(weight[g % 2][:, 0:stick_cols(g)], z_psum(g)[:, 0:stick_cols(g)],
                                     ACT.Exp).then_inc(w_done, 1)

            def o_upper(hp):
                wait_apart(act, fx_pv, STEPS * hp + STEPS)
                for kind in range(2):
                    nc.scalar.activation(o_tile(X[0], hp, kind), o_main[:, kind, :], ACT.Copy).then_inc(o_hi, 1)
                nc.scalar.activation(o_firsts(X[0], hp), o_first, ACT.Copy).then_inc(o_hi, 1)

            def act_drain():
                stick_weight(NH // 2 - 1, 7)
                o_upper(NH // 2 - 1)
            steps(act, act_step, act_drain)
            n1 = ph.n0 + 24
            nc.scalar.preload_act_table_set("sqrt_and_others")
            split(n1 + AHEAD, AHEAD)
            with act.Fori(0, 2) as i:
                for j in range(4):
                    n = n1 + 4 * i + j
                    split(n + AHEAD + 1, (j + AHEAD + 1) % RING)
                    wait_apart(act, drained, n + 1)
                    tail(4 * i + j, ph.x0 + 4 * i + j, A, ph.gain, 0)

        def attn_dve(dve, ph, split, tail, inverse, X, A):
            dve.wait_ge(wf_split, 1)
            nc.vector.tensor_tensor(wf_lo[:, :, :], wf_raw[:, :, :], wf_hi[:, :, :], ALU.subtract).then_inc(wf_split, 1)

            def group(i, first=False):
                for j in range(4):
                    n = ph.n0 + 4 * i + j
                    for ahead in splits_of(first, j):
                        split(n + ahead, (j + ahead) % RING)
                    if first and j == 0:
                        inverse(ph.s0, False)
                        dve.wait_ge(fg_mm, 1)
                        nc.vector.tensor_tensor(tok(fg, False), psum[2][0:NH, :, 0:HALF], tok(rinv[0:NH, :], False),
                                                ALU.mult).then_inc(fg_step, 1)
                    dve.wait_ge(unit_done, n + 1)
                    o = qkv[:, 4 * i + j, :]
                    sc = qkv_scale[:, i:i + 1] if isinstance(i, int) else qkv_scale[:, bass.ds(i, 1)]
                    nc.vector.scalar_tensor_tensor(tok(o, False), pair_of(j), sc, tok(rinv[:, :], False),
                                                   ALU.mult, ALU.mult).then_inc(drained, 1)
                    if first and j == 0:
                        dve.wait_ge(fg_step, 1)
                        nc.vector.tensor_scalar(fg, fg, bf_col[:, 0:1], None, ALU.add).then_inc(fg_step, 1)
                        nc.vector.memset(fg_one, 1.0).then_inc(fg_step, 1)
            group(0, True)
            dve.wait_ge(fg_act, 3)
            dve.wait_ge(fg_step, 3)
            nc.vector.scalar_tensor_tensor(fg, fg, 0.0, fg_abs, ALU.min, ALU.subtract).then_inc(fg_step, 1)
            dve.wait_ge(fg_step, 4)
            nc.vector.tensor_tensor_scan(fg_sum, fg_one, fg, 0.0, ALU.mult, ALU.add).then_inc(fg_step, 1)
            dve.wait_ge(fg_step, 5)
            nc.vector.tensor_scalar(fg_neg, fg_sum, -1.0, None, ALU.mult).then_inc(fg_step, 1)
            with dve.Fori(1, 6) as i:
                group(i)
            for r in range(0, QT, 2):
                v_turned_out(dve, r, nc.vector.tensor_copy)

            def dve_step(hp, g, first):
                e, s, c = g // 4, g % 4, STEPS * hp + g
                if g == 3 and not first:
                    o_lower(hp - 1)
                q0, nk = fox_tile(g)
                sc = s_psum(g)
                dve.wait_ge(s_done, c + 1)
                diag = sc[:, q0:q0 + P]
                nc.vector.tensor_tensor(diag, diag, causal[:, :], ALU.add).then_inc(s_masked, 1)
                if s == 0:
                    diag = sc[0:META, FIRST_S:FIRST_S + META]
                    nc.vector.tensor_tensor(diag, diag, causal[0:META, 0:META], ALU.add).then_inc(first_masked, 1)
                dve.wait_ge(s_masked, c + 1)
                nc.vector.tensor_reduce(stats[:, g % 2, 0:1], sc[:, 0:nk], AXX, ALU.max, negate=True).then_inc(max_done, 1)
                if s == 0:
                    dve.wait_ge(first_masked, 2 * hp + e + 1)
                    nc.vector.tensor_reduce(stats[0:META, 2, 0:1], diag, AXX, ALU.max, negate=True).then_inc(first_max, 1)
                w = stick_cols(g)
                dve.wait_ge(ln_done, c + 1)
                nc.vector.scalar_tensor_tensor(softplus[g % 2][:, 0:w], z_psum(g)[:, 0:w], 0.0, log1p[g % 2][:, 0:w],
                                               ALU.max, ALU.add).then_inc(sp_done, 1)
                if s > 0:
                    _, q1, nq = stick_tile(g - 1)
                    count_ge(dve, sticks_done, c)
                    dve.wait_ge(sp_masked, c)
                    dve.wait_ge(stick_ready, c)
                    if s == 1:
                        nc.vector.tensor_tensor(stick[:, SEQ:T], stick[:, SEQ:T], softplus[(g - 1) % 2][:, nq:nq + META],
                                                ALU.add).then_inc(stick_tail, 1)
                        dve.wait_ge(stick_tail, 2 * hp + e + 1)
                    nc.vector.tensor_tensor(stick[:, q1:T], stick[:, q1:T], softplus[(g - 1) % 2][:, 0:nq],
                                            ALU.add).then_inc(stick_ready, 1)
                t = before(hp, g, 1, first)
                if t is not None:
                    fox_turned(*t)
                dve.wait_ge(p_exp, c + 1)
                nc.vector.reciprocal(stats[:, g % 2, 2:3], stats[:, g % 2, 1:2]).then_inc(p_inv, 1)
                dve.wait_ge(p_inv, c + 1)
                p = probs[g % 2][:, 0:nk]
                nc.vector.tensor_scalar(p, p, stats[:, g % 2, 2:3], None, ALU.mult).then_inc(p_done, 1)
                if s == 0:
                    dve.wait_ge(first_exp, 2 * hp + e + 1)
                    nc.vector.reciprocal(stats[0:META, 2, 2:3], stats[0:META, 2, 1:2]).then_inc(first_inv, 1)
                    dve.wait_ge(first_inv, 2 * hp + e + 1)
                    nc.vector.tensor_scalar(first_probs[0:META, :], first_probs[0:META, :], stats[0:META, 2, 2:3], None,
                                            ALU.mult).then_inc(first_p, 1)
                if first and g == 0:
                    for r in range(QT + 1, 2 * QT, 2):
                        v_turned_out(dve, r, nc.vector.tensor_copy)

            def fox_turned(hp, g):
                s, c = g % 4, STEPS * hp + g
                dve.wait_ge(p_turned, c + 1)
                count_ge(dve, fx_pv, c - 1)
                src = s_psum(g)
                if s == 0:
                    nc.vector.tensor_copy(first_turned[0:META, :], src[0:META, FIRST_T:FIRST_T + META])
                if s == 3:
                    nc.vector.tensor_copy(turned_p[g % 2][0:META, 4, :], src[0:META, 4 * P:5 * P])
                full = min(s + 2, 4)
                nc.vector.tensor_copy(turned_p[g % 2][:, 0:full, :],
                                      src[:, 0:full * P].rearrange("p (b q) -> p b q", q=P)).then_inc(pt_out, 1)

            def o_lower(hp):
                for kind in range(2):
                    dve.wait_ge(o_hi, 3 * hp + kind + 1)
                    nc.vector.tensor_tensor(o_tile(X[1], hp, kind), o_main[:, kind, :], o_tile(X[0], hp, kind),
                                            ALU.subtract).then_inc(o_split, 1)
                dve.wait_ge(o_hi, 3 * hp + 3)
                nc.vector.tensor_tensor(o_firsts(X[1], hp), o_first, o_firsts(X[0], hp), ALU.subtract).then_inc(o_split, 1)

            def dve_drain():
                fox_turned(NH // 2 - 1, 7)
                o_lower(NH // 2 - 1)
            steps(dve, dve_step, dve_drain)
            n1 = ph.n0 + 24
            split(n1 + AHEAD, AHEAD)
            with dve.Fori(0, 2) as i:
                for j in range(4):
                    n = n1 + 4 * i + j
                    m = 4 * i + j
                    if j == 3:
                        split(n + AHEAD + 1, (j + AHEAD + 1) % RING)
                    dve.wait_ge(unit_done, n + 1)
                    hm = tok(h[:, m, :])
                    nc.vector.tensor_tensor(hm, pair_of(j), hm, ALU.add).then_inc(drained, 1)
                    if j < 3:
                        split(n + AHEAD + 1, (j + AHEAD + 1) % RING)
                    dve.wait_ge(drained, n + 1)
                    tail(m, ph.x0 + m, ph.xg0 + m, A, ph.gain, 0)

        def wait_apart(eng, sem_, count):
            if not isinstance(count, int):
                count = eng.to_reg(count)
            eng.wait_ge(consts, 8)
            eng.wait_ge(sem_, count)

        def splits_of(first, j):
            return [[3, 4], [4], [], []][j] if first else [AHEAD]

        def z_pair(a):
            return (a + 1) % 4

        @block.sync
        def _(sp):
            def fetch_x(c):
                cols = slice(c * 2 * P, (c + 1) * 2 * P)
                sp.dma_start(x_in[:, :, cols], x[0, :, cols].rearrange("(a p) d -> p a d", p=P)).then_inc(x_landed[c], 16)

            fetch_x(0)
            sp.dma_start(meta_in[:, :], meta_tokens).then_inc(meta_landed, 16)

            def strip(w, r0, nk, c0, width=P):
                return w[r0:r0 + nk * P, bass.ds(c0, width)].rearrange("(k p) c -> p k c", p=P)

            def dst(j, nk, width=P):
                return raw[j][:, 0:nk * width].rearrange("p (k c) -> p k c", c=width)

            def fetch_to(n, j, nk, src, width=P):
                if not isinstance(n, int) or n >= RING:
                    sp.wait_ge(lo_ready, n - RING + 1)
                sp.dma_start(dst(j, nk, width), src).then_inc(landed[j], 16)

            for ph in PHASES:
                if ph.kind == "ffn":
                    wi, wo = w_in[ph.which][ph.layer], w_out[ph.which][ph.layer]
                    for n0, t0, f0, nf in ph.blocks:
                        def in_group(i):
                            for j in range(4):
                                if isinstance(i, int) and n0 == 0 and j == 3:
                                    for c in range(1, 4):
                                        fetch_x(c)
                                c = (f0 + 2 * i + j // 2) * P + (j % 2) * FF
                                fetch_to(n0 + 4 * i + j, j, DK, strip(wi, 0, DK, c))
                        in_group(0)
                        with sp.Fori(1, nf // 2) as i:
                            in_group(i)
                        with sp.Fori(0, 2) as i:
                            for j in range(4):
                                fetch_to(n0 + 2 * nf + 4 * i + j, j, nf,
                                         strip(wo, f0 * P, nf, (4 * i + j) * P))
                elif ph.kind == "attn":
                    sp.dma_start(wf_raw[:, :, :], w_attn_in[0, :, 6 * SEQ:6 * SEQ + NH].rearrange("(k p) c -> p k c", p=P))\
                      .then_inc(fg_landed, 16)
                    sp.dma_start(bf_col[:, :], b_forget.rearrange("l h -> h l")).then_inc(fg_landed, 16)
                    with sp.Fori(0, 6) as i:
                        for j in range(4):
                            fetch_to(ph.n0 + 4 * i + j, j, DK, strip(w_attn_in[0], 0, DK, (4 * i + j) * P))
                    for i in range(2):
                        for j in range(4):
                            fetch_to(ph.n0 + 24 + 4 * i + j, j, DK, strip(w_attn_out[0], 0, DK, (4 * i + j) * P))
                        if i == 0:
                            stage_heads(sp, ph)
                else:
                    for j in range(4):
                        fetch_to(ph.n0 + j, j, 2, w_pool[0, j].rearrange("(k p) c -> p k c", p=P), 2 * P)
            for t in range(SEQ // P):
                for half, done in ((0, y_first), (1, y_second)):
                    cols = slice(half * 512, (half + 1) * 512)
                    sp.wait_ge(done, t + 1)
                    sp.dma_start(out[0, t * P:(t + 1) * P, cols], y_out[:, t, cols]).then_inc(y_stored, 16)
            sp.wait_ge(y_stored, 32 * (SEQ // P))

        def land_wait(eng, n, j):
            eng.wait_ge(landed[j], (n - j) * (16 // RING) + 16)

        @block.scalar
        def _(act):
            act.dma_start(first_rows[:, :], g_ffn1.rearrange("l (m p) -> (l m) p", p=P)).then_inc(first_landed, 16)
            act.dma_start(gain_rows[0:16, :], g_mix.rearrange("l (m p) -> (l m) p", p=P)).then_inc(rows_landed, 16)
            act.dma_start(gain_rows[16:32, :], g_ffn2.rearrange("l (m p) -> (l m) p", p=P)).then_inc(rows_landed, 16)
            act.dma_start(gain_rows[32:40, :], g_final.rearrange("(m p) -> m p", p=P)).then_inc(rows_landed, 16)
            act.dma_start(gain_rows[40:48, :], pool_scale.rearrange("l (m p) -> (l m) p", p=P)).then_inc(rows_landed, 16)

            def split(n, j):
                if isinstance(n, int) and n >= UNITS:
                    return
                land_wait(act, n, j)
                if not isinstance(n, int) or n >= RING:
                    act.wait_ge(unit_done, n - RING + 1)
                nc.scalar.activation(w_hi[j][:, :], raw[j][:, :], ACT.Copy).then_inc(hi_ready, 1)

            def tail(m, x1, X, gain, lo):
                v = h[:, m, lo:T]
                if gain is not None:
                    nc.scalar.activation(X[0][:, m, lo:T], v, ACT.Copy,
                                         scale=gains[:, gain * DK + m:gain * DK + m + 1] if isinstance(m, int)
                                         else gains[:, bass.ds(m + gain * DK, 1)]).then_inc(xg_hi_ready, 1)
                elif lo:
                    nc.scalar.activation(y_gained[:, m * SEQ:(m + 1) * SEQ], v, ACT.Copy,
                                         scale=gains[:, G_FINAL * DK + m:G_FINAL * DK + m + 1]).then_inc(scaled, 1)
                wait_apart(act, sq_added, x1)
                nc.scalar.activation(sq[:, lo:T], v, ACT.Square).then_inc(sq_ready, 1)

            def root(s, last):
                act.wait_ge(sums_done, s + 1)
                lo = META if last else 0
                nc.scalar.activation(tok(sq[:, :], last), pair_of(3, last), ACT.Sqrt, scale=1.0 / D,
                                     bias=eps_col[:, 0:1]).then_inc(root_ready, 1)

            act.wait_ge(consts, 8)
            nc.scalar.preload_act_table_set("sqrt_and_others")
            split(0, 0)
            act.wait_ge(gains_ready, 1)
            act.wait_ge(meta_drained, 1)
            for m in range(DK):
                act.wait_ge(x_drained, m + 1)
                tail(m, m, B[0], G_FFN1[0], 0)
                if m == 0:
                    split(1, 1)
                    split(2, 2)

            for ph in PHASES:
                X, A = B[ph.swapped], B[not ph.swapped]
                lo = META if ph.last else 0
                if ph.kind == "ffn":
                    for b, (n0, t0, f0, nf) in enumerate(ph.blocks):
                        def in_group(i, first=False):
                            for j in range(4):
                                n = n0 + 4 * i + j
                                for ahead in splits_of(first, j):
                                    split(n + ahead, (j + ahead) % RING)
                                if first and j == 0:
                                    root(ph.s0, ph.last)
                                if j % 2 == 0:
                                    act.wait_ge(drained, n + 1)
                                    nc.scalar.activation(silu[:, lo:T], gate[:, lo:T], ACT.Silu).then_inc(silu_ready, 1)
                                else:
                                    f = 2 * i + j // 2
                                    wait_apart(act, hid_ready, t0 + f + 1)
                                    nc.scalar.activation(A[0][:, f, lo:T], hid[:, lo:T], ACT.Copy).then_inc(act_hi_ready, 1)
                        in_group(0, first=b == 0)
                        with act.Fori(1, nf // 2) as i:
                            in_group(i)
                        n1 = n0 + 2 * nf
                        final = b == len(ph.blocks) - 1
                        if final:
                            nc.scalar.preload_act_table_set("sqrt_and_others")
                            split(n1 + AHEAD, AHEAD)

                        def out_group(i):
                            for j in range(4):
                                n = n1 + 4 * i + j
                                ahead = AHEAD + final
                                split(n + ahead, (j + ahead) % RING)
                                if final:
                                    wait_apart(act, drained, n + 1)
                                    tail(4 * i + j, ph.x0 + 4 * i + j, X, ph.gain, lo)
                        if final and ph.last:
                            out_group(0)
                            out_group(1)
                        else:
                            with act.Fori(0, 2) as i:
                                out_group(i)
                elif ph.kind == "attn":
                    attn_act(act, ph, split, tail, root, X, A)
                else:
                    split(ph.n0 + 3, 3)
                    act.wait_ge(sums_done, ph.s0 + 1)
                    nc.scalar.activation(root_col[:, 0:4], psum[0][:, 0, 0:4], ACT.Sqrt, scale=1.0 / D, bias=eps_col[:, 0:1])
                    nc.scalar.activation(root_col[0:META, 4:5], psum[0][0:META, 0, 4:5], ACT.Sqrt, scale=1.0 / D,
                                         bias=eps_col[0:META, 0:1]).then_inc(root_ready, 1)
                    act.wait_ge(rinv_ready, ph.s0 + 1)
                    for a in range(QT):
                        _, kn = key_tile(a)
                        if a < QT - 1:
                            act.wait_ge(z_turned, a + 1)
                        else:
                            act.wait_ge(unit_done, ph.n0 + 4)
                        nc.scalar.activation(z_tok[0:kn, a, 0:512], psum[z_pair(a)][0:kn, 0, :], ACT.Copy,
                                             scale=rinv_col[0:kn, a:a + 1]).then_inc(z_first, 1)
                    for ahead in range(4, 7):
                        split(ph.n0 + ahead, ahead % RING)
                    for m in range(DK):
                        if m % 2 == 0:
                            act.wait_ge(pool_added, m // 2 + 1)
                        else:
                            act.wait_ge(drained, ph.n0 + m // 2 + 1)
                        tail(m, ph.x0 + m, A, ph.gain, META)
            act.wait_ge(y_turned, 4)
            nc.scalar.activation(y_out[:, 3, 0:512], psum[3][:, 1, :], ACT.Copy).then_inc(y_apart, 1)
            act.wait_ge(sums_done, len(PHASES) + 1)
            nc.scalar.activation(root_col[:, 0:4], psum[3][:, 1, 0:4], ACT.Sqrt, scale=1.0 / D,
                                 bias=eps_col[:, 0:1]).then_inc(root_ready, 1)
            act.wait_ge(rinv_ready, len(PHASES) + 1)
            for t in range(SEQ // P):
                src = psum[t][:, 1, :] if t < 3 else y_out[:, 3, 0:512]
                nc.scalar.activation(y_out[:, t, 0:512], src, ACT.Copy, scale=rinv_col[:, t:t + 1]).then_inc(y_first, 1)

        @block.vector
        def _(dve):
            def split(n, j):
                if isinstance(n, int) and n >= UNITS:
                    return
                dve.wait_ge(hi_ready, n + 1)
                nc.vector.tensor_tensor(w_lo[j][:, :], raw[j][:, :], w_hi[j][:, :], ALU.subtract).then_inc(lo_ready, 1)

            def tail_gained(m, xg1, X, gain, lo):
                if gain is not None:
                    dve.wait_ge(xg_hi_ready, xg1 + 1)
                    g = gains[:, gain * DK + m:gain * DK + m + 1] if isinstance(m, int) else gains[:, bass.ds(m + gain * DK, 1)]
                    nc.vector.scalar_tensor_tensor(X[1][:, m, lo:T], h[:, m, lo:T], g, X[0][:, m, lo:T],
                                                   ALU.mult, ALU.subtract).then_inc(xg_ready, 1)

            def tail_sum(x1, lo):
                dve.wait_ge(sq_ready, x1 + 1)
                dve.wait_ge(sq_added, x1)
                nc.vector.tensor_tensor(sumsq[:, lo:T], sumsq[:, lo:T], sq[:, lo:T], ALU.add).then_inc(sq_added, 1)

            def tail(m, x1, xg1, X, gain, lo):
                tail_gained(m, xg1, X, gain, lo)
                tail_sum(x1, lo)

            def inverse(s, last):
                dve.wait_ge(root_ready, s + 1)
                lo = META if last else 0
                nc.vector.reciprocal(rinv[:, lo:T], sq[:, lo:T]).then_inc(rinv_ready, 1)
                nc.vector.memset(sumsq[:, :], 0.0).then_inc(zeroed, 1)
                dve.wait_ge(rinv_ready, s + 1)
                dve.wait_ge(zeroed, s + 2)

            nc.vector.memset(sumsq[:, :], 0.0).then_inc(zeroed, 1)
            dve.wait_ge(zeroed, 1)
            dve.wait_ge(gains_t, 1)
            nc.vector.tensor_copy(gains[:, 0:2 * DK], psum[2][:, 0, 0:2 * DK]).then_inc(gains_ready, 1)
            dve.wait_ge(meta_turned, 1)
            nc.vector.tensor_copy(h[:, :, 0:META], psum[2][:, 1, 0:DK * META].rearrange("p (m t) -> p m t", m=DK))\
              .then_inc(meta_drained, 1)

            def evacuate_x(m):
                dve.wait_ge(turned, m + 1)
                nc.vector.tensor_copy(h[:, m, META:T], psum[3][:, m % 2, :]).then_inc(x_drained, 1)

            evacuate_x(0)
            dve.wait_ge(gains_ready, 1)
            dve.wait_ge(meta_drained, 1)
            split(0, 0)
            tail_gained(0, 0, B[0], G_FFN1[0], 0)
            split(1, 1)
            dve.wait_ge(gains_t, 2)
            nc.vector.tensor_copy(gains[:, 2 * DK:8 * DK], psum[2][:, 0, 2 * DK:8 * DK]).then_inc(gains_ready, 1)
            split(2, 2)
            evacuate_x(1)
            tail_sum(0, 0)
            for m in range(1, DK):
                dve.wait_ge(x_drained, m + 1)
                tail_gained(m, m, B[0], G_FFN1[0], 0)
                if m + 1 < DK:
                    evacuate_x(m + 1)
                tail_sum(m, 0)

            for ph in PHASES:
                X, A = B[ph.swapped], B[not ph.swapped]
                lo = META if ph.last else 0
                if ph.kind == "ffn":
                    for b, (n0, t0, f0, nf) in enumerate(ph.blocks):
                        def in_group(i, first=False):
                            for j in range(4):
                                n = n0 + 4 * i + j
                                for ahead in splits_of(first, j):
                                    split(n + ahead, (j + ahead) % RING)
                                if first and j == 0:
                                    inverse(ph.s0, ph.last)
                                dve.wait_ge(unit_done, n + 1)
                                f = 2 * i + j // 2
                                if j % 2 == 0:
                                    nc.vector.tensor_tensor(tok(gate[:, :], ph.last), pair_of(j, ph.last),
                                                            tok(rinv[:, :], ph.last), ALU.mult).then_inc(drained, 1)
                                else:
                                    count_ge(dve, act_ready, t0 + f)
                                    nc.vector.tensor_tensor(tok(hid[:, :], ph.last), pair_of(j, ph.last),
                                                            tok(rinv[:, :], ph.last), ALU.mult).then_inc(drained, 1)
                                    dve.wait_ge(silu_ready, t0 + f + 1)
                                    dve.wait_ge(drained, n + 1)
                                    nc.vector.tensor_tensor(hid[:, lo:T], hid[:, lo:T], silu[:, lo:T],
                                                            ALU.mult).then_inc(hid_ready, 1)
                                    dve.wait_ge(act_hi_ready, t0 + f + 1)
                                    nc.vector.tensor_tensor(A[1][:, f, lo:T], hid[:, lo:T], A[0][:, f, lo:T],
                                                            ALU.subtract).then_inc(act_ready, 1)
                        in_group(0, first=b == 0)
                        with dve.Fori(1, nf // 2) as i:
                            in_group(i)
                        n1 = n0 + 2 * nf
                        final = b == len(ph.blocks) - 1
                        if final:
                            split(n1 + AHEAD, AHEAD)

                        def out_group(i):
                            for j in range(4):
                                n = n1 + 4 * i + j
                                m = 4 * i + j
                                if not final:
                                    split(n + AHEAD, (j + AHEAD) % RING)
                                elif j == 3:
                                    split(n + AHEAD + 1, (j + AHEAD + 1) % RING)
                                dve.wait_ge(unit_done, n + 1)
                                hm = tok(h[:, m, :], ph.last)
                                nc.vector.scalar_tensor_tensor(hm, pair_of(j, ph.last), 0.5, hm,
                                                               ALU.mult, ALU.add).then_inc(drained, 1)
                                if final:
                                    if j < 3:
                                        split(n + AHEAD + 1, (j + AHEAD + 1) % RING)
                                    dve.wait_ge(drained, n + 1)
                                    tail(m, ph.x0 + m, xg_base(ph) + m, X, ph.gain, lo)
                        if final and ph.last:
                            out_group(0)
                            out_group(1)
                        else:
                            with dve.Fori(0, 2) as i:
                                out_group(i)
                elif ph.kind == "attn":
                    attn_dve(dve, ph, split, tail, inverse, X, A)
                else:
                    split(ph.n0 + 3, 3)
                    dve.wait_ge(root_ready, ph.s0 + 1)
                    nc.vector.reciprocal(rinv_col[:, 0:4], root_col[:, 0:4])
                    nc.vector.reciprocal(rinv_col[0:META, 4:5], root_col[0:META, 4:5]).then_inc(rinv_ready, 1)
                    nc.vector.memset(sumsq[:, :], 0.0).then_inc(zeroed, 1)
                    dve.wait_ge(rinv_ready, ph.s0 + 1)
                    for a in range(QT):
                        _, kn = key_tile(a)
                        if a < QT - 1:
                            dve.wait_ge(z_turned, a + 1)
                        else:
                            dve.wait_ge(unit_done, ph.n0 + 4)
                        nc.vector.tensor_scalar(z_tok[0:kn, a, 512:D], psum[z_pair(a)][0:kn, 1, :],
                                                rinv_col[0:kn, a:a + 1], None, ALU.mult).then_inc(z_second, 1)
                    for ahead in range(4, 7):
                        split(ph.n0 + ahead, ahead % RING)
                    dve.wait_ge(zeroed, ph.s0 + 2)

                    def add_pooled(m):
                        dve.wait_ge(pool_done, m + 1)
                        nc.vector.scalar_tensor_tensor(
                            h[:, m, META:T], psum[m // 2][:, m % 2, :], gains[:, G_POOL * DK + m:G_POOL * DK + m + 1],
                            h[:, m, META:T], ALU.mult, ALU.add).then_inc(drained if m % 2 else pool_added, 1)

                    for m in range(6):
                        add_pooled(m)
                    for m in range(DK):
                        if m % 2:
                            dve.wait_ge(drained, ph.n0 + m // 2 + 1)
                        else:
                            dve.wait_ge(pool_added, m // 2 + 1)
                        tail(m, ph.x0 + m, xg_base(ph) + m, A, ph.gain, META)
                        if m + 6 < DK:
                            add_pooled(m + 6)
            dve.wait_ge(root_ready, len(PHASES) + 1)
            nc.vector.reciprocal(rinv_col[:, 0:4], root_col[:, 0:4]).then_inc(rinv_ready, 1)
            dve.wait_ge(rinv_ready, len(PHASES) + 1)
            for t in range(SEQ // P):
                dve.wait_ge(y_turned, 4 + t + 1)
                nc.vector.tensor_scalar(y_out[:, t, 512:D], psum[t][:, 0, :], rinv_col[:, t:t + 1], None,
                                        ALU.mult).then_inc(y_second, 1)

        @block.tensor
        def _(pe):
            def product(n, j, nk, rhs, last, ready=None, ready0=0):
                pe.wait_ge(lo_ready, n + 1)
                if not isinstance(n, int) or n >= RING:
                    pe.wait_ge(drained, n - RING + 1)
                for k in range(nk):
                    if ready is not None:
                        pe.wait_ge(ready, ready0 + k + 1)
                    blk = slice(k * P, (k + 1) * P)
                    for w, v in ((w_hi, 0), (w_hi, 1), (w_lo, 0)):
                        for bank, c0, cols, t0 in halves(last):
                            mm = nc.tensor.matmul(psum[j][:, bank, c0:c0 + cols], w[j][:, blk],
                                                  rhs[v][:, k, t0:t0 + cols],
                                                  start=(k == 0 and w is w_hi and v == 0),
                                                  stop=(k == nk - 1 and w is w_lo))
                mm.then_inc(unit_done, 1)

            def turn_y(m, tiles, bank):
                pe.wait_ge(scaled, m + 1)
                for a in tiles:
                    mm = nc.tensor.transpose(psum[a][:, bank, (m % 4) * P:(m % 4 + 1) * P],
                                             y_gained[:, m * SEQ + a * P:m * SEQ + (a + 1) * P], ident[:, :])
                    if m % 4 == 3:
                        mm.then_inc(y_turned, 1)

            def pool_pe(ph, X):
                n0 = ph.n0

                def by_token(a, g):
                    t, kn = key_tile(a)
                    for k in range(2):
                        for v, w in ((0, w_hi), (0, w_lo), (1, w_hi)):
                            mm = nc.tensor.matmul(
                                psum[z_pair(a)][0:kn, g // 2, g % 2 * 2 * P:(g % 2 + 1) * 2 * P],
                                X[v][:, 2 * g + k, t:t + kn], w[g][:, k * 2 * P:(k + 1) * 2 * P],
                                start=(k == 0 and v == 0 and w is w_hi), stop=(k == 1 and v == 1))
                    return mm

                for g in range(4):
                    pe.wait_ge(lo_ready, n0 + g + 1)
                    pe.wait_ge(xg_ready, xg_base(ph) - DK + 2 * g + 2)
                    for a in range(2):
                        if g == 0:
                            pe.wait_ge(drained, n0 - 4 + z_pair(a) + 1)
                        mm = by_token(a, g)
                        if g == 3:
                            mm.then_inc(z_turned, 1)
                pe.wait_ge(sq_added, ph.x0)
                for a in range(QT):
                    t, kn = key_tile(a)
                    mm = nc.tensor.matmul(psum[0][0:kn, 0, a:a + 1], sumsq[:, t:t + kn], ones[:, 0:1],
                                          start=True, stop=True)
                mm.then_inc(sums_done, 1)
                for a in range(2, QT):
                    if a == 2:
                        pe.wait_ge(drained, n0)
                    elif a == 3:
                        pe.wait_ge(root_ready, ph.s0 + 1)
                    else:
                        pe.wait_ge(z_first, 1)
                        pe.wait_ge(z_second, 1)
                    for g in range(4):
                        mm = by_token(a, g)
                        if a == QT - 1:
                            mm.then_inc(unit_done, 1)
                    if a < QT - 1:
                        mm.then_inc(z_turned, 1)
                pe.wait_ge(bands, 4 * len(WINDOWS))
                for m in range(DK):
                    b = band[:, m * P * len(WINDOWS) // D, :]
                    for a in range(QT):
                        t, kn = key_tile(a)
                        if m == 0 or m == 4:
                            pe.wait_ge(z_first if m == 0 else z_second, a + 1)
                        if m == 0 and a == 0:
                            pe.wait_ge(z_first, 4)
                            pe.wait_ge(z_second, 4)
                        if m == 2 and a == 0:
                            pe.wait_ge(z_second, QT)
                        c0 = max(t - META, 0)
                        b0 = META if a == 0 else 0
                        cols = min(BAND - b0, SEQ - c0)
                        mm = nc.tensor.matmul(psum[m // 2][:, m % 2, c0:c0 + cols], z_tok[0:kn, a, m * P:(m + 1) * P],
                                              b[0:kn, b0:b0 + cols], start=(a == 0), stop=True, skip_group_check=True)
                    mm.then_inc(pool_done, 1)

            def sums(s, x1, n, last):
                pe.wait_ge(sq_added, x1)
                if n > 0:
                    pe.wait_ge(drained, n)
                for bank, c0, cols, t0 in halves(last):
                    mm = nc.tensor.matmul(psum[3][:, bank, c0:c0 + cols], ones[:, :], sumsq[:, t0:t0 + cols],
                                          start=True, stop=True)
                mm.then_inc(sums_done, 1)

            pe.wait_ge(consts, 8)
            pe.wait_ge(consts2, 1)
            def turn_x(m):
                if m % 2 == 0:
                    pe.wait_ge(x_landed[m // 2], 16)
                if m >= 2:
                    pe.wait_ge(x_drained, m - 1)
                for a in range(SEQ // P):
                    mm = nc.tensor.transpose(psum[3][:, m % 2, a * P:(a + 1) * P], x_in[:, a, m * P:(m + 1) * P], ident[:, :])
                mm.then_inc(turned, 1)

            turn_x(0)
            pe.wait_ge(first_landed, 16)
            nc.tensor.transpose(psum[2][:, 0, 0:2 * DK], first_rows[:, :], ident[0:2 * DK, 0:2 * DK]).then_inc(gains_t, 1)
            pe.wait_ge(meta_landed, 16)
            for m in range(DK):
                mm = nc.tensor.transpose(psum[2][:, 1, m * META:(m + 1) * META], meta_in[:, m * P:(m + 1) * P],
                                         ident[0:META, 0:META])
            mm.then_inc(meta_turned, 1)
            turn_x(1)
            pe.wait_ge(rows_landed, 64)
            pe.wait_ge(gains_ready, 1)
            nc.tensor.transpose(psum[2][:, 0, 2 * DK:8 * DK], gain_rows[:, :], ident[0:6 * DK, 0:6 * DK]).then_inc(gains_t, 1)
            pe.wait_ge(gains_ready, 2)
            pe.wait_ge(meta_drained, 1)

            def first_three(ph, X):
                for j in range(3):
                    pe.wait_ge(lo_ready, ph.n0 + j + 1)
                    if ph.n0 > 0:
                        pe.wait_ge(drained, ph.n0 + j - RING + 1)
                for k in range(DK):
                    pe.wait_ge(xg_ready, xg_base(ph) - DK + k + 1)
                    if ph.n0 == 0 and k + 2 < DK:
                        turn_x(k + 2)
                    blk = slice(k * P, (k + 1) * P)
                    for j in range(3):
                        for w, v in ((w_hi, 0), (w_hi, 1), (w_lo, 0)):
                            for bank, c0, cols, t0 in halves(ph.last):
                                mm = nc.tensor.matmul(psum[j][:, bank, c0:c0 + cols], w[j][:, blk],
                                                      X[v][:, k, t0:t0 + cols],
                                                      start=(k == 0 and w is w_hi and v == 0),
                                                      stop=(k == DK - 1 and w is w_lo))
                        if k == DK - 1:
                            mm.then_inc(unit_done, 1)
                            if j == 0:
                                sums(ph.s0, ph.x0, ph.n0, ph.last)

            for ph in PHASES:
                X, A = B[ph.swapped], B[not ph.swapped]
                if ph.kind == "ffn":
                    for b, (n0, t0, f0, nf) in enumerate(ph.blocks):
                        def in_group(i, first=False):
                            if first:
                                first_three(ph, X)
                                pe.wait_ge(root_ready, ph.s0 + 1)
                            for j in range(3 if first else 0, 4):
                                product(n0 + 4 * i + j, j, DK, X, ph.last)
                        in_group(0, first=b == 0)
                        with pe.Fori(1, nf // 2) as i:
                            in_group(i)
                        n1 = n0 + 2 * nf
                        if ph.last and b == len(ph.blocks) - 1:
                            for m in range(DK):
                                product(n1 + m, m % 4, nf, A, True, act_ready if m == 0 else None, t0)
                                if 1 <= m <= 4:
                                    turn_y(m - 1, range(4), 1)
                        else:
                            with pe.Fori(0, 2) as i:
                                for j in range(4):
                                    product(n1 + 4 * i + j, j, nf, A, ph.last, act_ready if j == 0 else None, t0)
                elif ph.kind == "attn":
                    attn_pe(pe, ph, product, sums, X, A)
                else:
                    pool_pe(ph, X)
            for a in range(SEQ // P):
                pe.wait_ge(drained, UNITS - 4 + a + 1)
                for m in range(4, 7):
                    turn_y(m, [a], 0)
            turn_y(7, range(4), 0)
            pe.wait_ge(y_apart, 1)
            pe.wait_ge(sq_added, FINAL_X + DK)
            for t in range(SEQ // P):
                mm = nc.tensor.matmul(psum[3][:, 1, t:t + 1], sumsq[:, META + t * P:META + (t + 1) * P], ones[:, 0:1],
                                      start=True, stop=True)
            mm.then_inc(sums_done, 1)

        @block.gpsimd
        def _(pool):
            for t in (ident, neg_tri, causal):
                nc.gpsimd.memset(t[:, :], {id(ident): 0.0, id(neg_tri): -1.0, id(causal): 0.0}[id(t)]).then_inc(consts, 1)
            nc.gpsimd.memset(ones[:, :], 1.0).then_inc(consts, 1)
            nc.gpsimd.memset(neg_ones[:, :], -1.0).then_inc(consts, 1)
            nc.gpsimd.memset(eps_col[:, :], EPS).then_inc(consts, 1)
            nc.gpsimd.memset(qkv_scale[:, :], 1.0).then_inc(consts, 1)
            pool.wait_ge(consts, 7)
            nc.gpsimd.memset(qkv_scale[:, 0:4:3], SCALE).then_inc(consts, 1)
            nc.gpsimd.affine_select(out=ident[:, :], in_=ident[:, :], compare_op=ALU.not_equal, fill=1.0, base=0,
                                    pattern=[[-1, P]], channel_multiplier=1).then_inc(consts2, 1)
            nc.gpsimd.affine_select(out=neg_tri[:, :], in_=neg_tri[:, :], compare_op=ALU.is_ge, fill=0.0, base=0,
                                    pattern=[[-1, P]], channel_multiplier=1).then_inc(consts2, 1)
            nc.gpsimd.affine_select(out=causal[:, :], in_=causal[:, :], compare_op=ALU.is_ge, fill=MASKED, base=0,
                                    pattern=[[-1, P]], channel_multiplier=1).then_inc(consts2, 1)
            for ph in PHASES:
                if ph.kind != "attn":
                    continue
                pool.wait_ge(drained, ph.n0 + 1)
                nc.gpsimd.memset(v_tok[:, :, QT - 1, :], 0.0).then_inc(v_pad, 1)
                pool.wait_ge(fg_step, 6)
                pool.dma_start(c_dram[0], fg_sum).then_inc(c_stored, 16)
                pool.dma_start(c_dram[1], fg_neg).then_inc(c_stored, 16)
                pool.wait_ge(v_pad, 1)
                for e in range(2):
                    nc.gpsimd.memset(fx_q[e][HD:HD + 2, :], 1.0).then_inc(aug_ones, 1)
                    nc.gpsimd.memset(fx_k[e][HD:HD + 2, :], 1.0).then_inc(aug_ones, 1)
                pool.wait_ge(aug_ones, 4)
                for e in range(2):
                    nc.gpsimd.memset(sb_k[e][:, T:SEQ + P], 0.0).then_inc(aug_ones, 1)
                nc.gpsimd.memset(first_probs[:, :], 0.0).then_inc(first_zero, 1)

                def mask(t, g, done):
                    _, q0, nq = stick_tile(g)
                    if g % 4 == 0:
                        both = t[:, nq:nq + 2 * META].rearrange("p (a b) -> p a b", a=2)
                        nc.gpsimd.affine_select(out=both, in_=both, compare_op=ALU.is_gt, fill=0.0, base=0,
                                                pattern=[[0, 2], [1, META]], channel_multiplier=-1)
                    ahead = META if g % 4 == 3 else 0
                    own = t[:, 0:P - ahead]
                    nc.gpsimd.affine_select(out=own, in_=own, compare_op=ALU.is_gt, fill=0.0, base=ahead,
                                            pattern=[[1, P - ahead]], channel_multiplier=-1).then_inc(done, 1)

                def weight_mask(hp, g):
                    wait_apart(pool, w_done, STEPS * hp + g + 1)
                    mask(weight[g % 2], g, w_masked)

                def pool_step_(hp, g, first):
                    wait_apart(pool, sp_done, STEPS * hp + g + 1)
                    mask(softplus[g % 2], g, sp_masked)
                    t = before(hp, g, 1, first)
                    if t is not None:
                        weight_mask(*t)
                    if g % 4 == 0:
                        if first and g == 0:
                            pool.wait_ge(vt_turned, 2 * QT)
                        else:
                            wait_apart(pool, sticks_done, STEPS * hp + g)
                        nc.gpsimd.memset(stick, 0.0).then_inc(stick_ready, 1)
                steps(pool, pool_step_, lambda: weight_mask(NH // 2 - 1, 7))
                pool.wait_ge(drained, ph.n0 + 24 + DK + 1)
                for i, w in enumerate(WINDOWS):
                    b = band[:, i, :]
                    nc.gpsimd.memset(b, 1.0 / w).then_inc(bands, 1)
                    pool.wait_ge(bands, 4 * i + 1)
                    nc.gpsimd.affine_select(out=b, in_=b, compare_op=ALU.is_ge, fill=0.0, base=0,
                                            pattern=[[1, BAND]], channel_multiplier=-1).then_inc(bands, 1)
                    pool.wait_ge(bands, 4 * i + 2)
                    nc.gpsimd.affine_select(out=b, in_=b, compare_op=ALU.is_ge, fill=0.0, base=w - 1,
                                            pattern=[[-1, BAND]], channel_multiplier=1).then_inc(bands, 1)
                    pool.wait_ge(bands, 4 * i + 3)
                    nc.gpsimd.affine_select(out=b, in_=b, compare_op=ALU.not_equal, fill=1.0 / w - 1.0, base=0,
                                            pattern=[[-1, BAND]], channel_multiplier=1).then_inc(bands, 1)


_INS = ["x", "meta_tokens", "g_ffn1", "w_ffn1_in", "w_ffn1_out", "g_mix", "g_ffn2", "w_ffn2_in", "w_ffn2_out",
        "w_attn_in", "b_forget", "w_attn_out", "w_pool", "pool_scale", "g_final"]


def kernel(**inputs):
    import concourse.bacc as bacc
    from concourse.bass_utils import run_bass_kernel_spmd

    nc = bacc.Bacc("TRN2", target_bir_lowering=False, num_devices=1)
    arrays, args = {}, []
    for name in _INS:
        a = np.ascontiguousarray(inputs[name])
        arrays[f"in_{name}"] = a
        args.append(nc.dram_tensor(f"in_{name}", a.shape, mybir.dt.from_np(a.dtype), kind="ExternalInput").ap())
    out = nc.dram_tensor("out_y", (1, SEQ, D), F32, kind="ExternalOutput").ap()
    trunk(nc, *args, out)
    r = run_bass_kernel_spmd(nc, [arrays], core_ids=[0])
    return r.results[0]["out_y"]
```
